# Optimizing a Trainium2 kernel written in Bass

```python
import math
import jax
import jax.numpy as jnp
from jax import lax
import numpy as np

D_MODEL = 1024
BATCH = 1
SEQ = 512
DEPTH = 1

SSD_D_INNER = 1024
SSD_HEADDIM = 64
SSD_HEADS = SSD_D_INNER // SSD_HEADDIM
SSD_GROUPS = 2
SSD_HPG = SSD_HEADS // SSD_GROUPS
SSD_STATE = 128
CONV_WIDTH = 3
CHUNK = 128
SSD_CONV_DIM = SSD_D_INNER + 2 * SSD_GROUPS * SSD_STATE

MLA_HEADS = 16
QK_NOPE = 64
QK_ROPE = 32
V_HEAD = 64
Q_LORA = 384
KV_LORA = 256
Q_BLOCK = 128
ROPE_THETA = 10000.0

PEER_HEADS = 8
N_KEYS = 128
N_EXPERTS = N_KEYS * N_KEYS
KEY_HALF = 128
PEER_TOPK = 16
TOK_BLOCK = 128

EPS = 1e-6

IN_SIZES = (SSD_D_INNER, SSD_CONV_DIM, 2 * SSD_HEADS, Q_LORA, KV_LORA, QK_ROPE, 2 * D_MODEL)
IN_COLS = sum(IN_SIZES)

kernel_name = "hybrid_ssd_mla_peer_block"

def _split_points(sizes):
    pts, acc = [], 0
    for s in sizes[:-1]:
        acc += s
        pts.append(acc)
    return pts

def rms_norm(x, w):
    xf = x.astype(jnp.float32)
    y = xf * lax.rsqrt(jnp.mean(xf * xf, axis=-1, keepdims=True) + EPS)
    return (y * w.astype(jnp.float32)).astype(x.dtype)

def depthwise_conv_centred(x, w, b):
    c = x.shape[-1]
    k = w.shape[0]
    y = lax.conv_general_dilated(x, w[:, None, :], window_strides=(1,),
                                 padding=[(k // 2, k // 2)],
                                 dimension_numbers=('NWC', 'WIO', 'NWC'),
                                 feature_group_count=c)
    return y + b

def segsum(a):
    t = a.shape[-1]
    cs = jnp.cumsum(a, axis=-1)
    diff = cs[..., :, None] - cs[..., None, :]
    mask = jnp.tril(jnp.ones((t, t), dtype=bool))
    return jnp.where(mask, diff, -jnp.inf)

def ssd_scan(xh, dt, A, Bm, Cm):
    b, l, g, r, p = xh.shape
    n = Bm.shape[-1]
    c = l // CHUNK
    f32 = jnp.float32
    xd = (xh.astype(f32) * dt.astype(f32)[..., None]).reshape(b, c, CHUNK, g, r, p)
    a = (dt.astype(f32) * A.astype(f32)).reshape(b, c, CHUNK, g, r)
    a = jnp.moveaxis(a, 2, -1)
    Bc = Bm.astype(f32).reshape(b, c, CHUNK, g, n)
    Cc = Cm.astype(f32).reshape(b, c, CHUNK, g, n)
    a_cs = jnp.cumsum(a, axis=-1)
    L = jnp.exp(segsum(a))
    CB = jnp.einsum('bclgn,bcsgn->bcgls', Cc, Bc)
    y_diag = jnp.einsum('bcgls,bcgrls,bcsgrp->bclgrp', CB, L, xd)
    decay_states = jnp.exp(a_cs[..., -1:] - a_cs)
    states = jnp.einsum('bcsgn,bcgrs,bcsgrp->bcgrpn', Bc, decay_states, xd)
    chunk_tot = jnp.moveaxis(a_cs[..., -1], 1, -1)
    decay_chunk = jnp.exp(segsum(jnp.pad(chunk_tot, ((0, 0), (0, 0), (0, 0), (1, 0)))))
    states0 = jnp.pad(states, ((0, 0), (1, 0), (0, 0), (0, 0), (0, 0), (0, 0)))
    new_states = jnp.einsum('bgrzc,bcgrpn->bzgrpn', decay_chunk, states0)
    prev = new_states[:, :-1]
    state_decay_out = jnp.exp(a_cs)
    y_off = jnp.einsum('bclgn,bcgrpn,bcgrl->bclgrp', Cc, prev, state_decay_out)
    return (y_diag + y_off).reshape(b, l, g, r, p)

def rope_tables(positions, dim, dtype):
    inv = 1.0 / (ROPE_THETA ** (jnp.arange(0, dim, 2, dtype=jnp.float32) / dim))
    ang = positions.astype(jnp.float32)[..., None] * inv
    return jnp.cos(ang).astype(dtype), jnp.sin(ang).astype(dtype)

def apply_rope(x, cos, sin):
    x1, x2 = jnp.split(x, 2, axis=-1)
    return jnp.concatenate([x1 * cos - x2 * sin, x1 * sin + x2 * cos], axis=-1)

def mla_attention(q_nope, q_rope, k_nope, k_rope, v):
    b, s, h, _ = q_nope.shape
    nb = s // Q_BLOCK
    scale = (QK_NOPE + QK_ROPE) ** -0.5

    def block(args):
        qn, qr = args
        sc = (jnp.einsum('bqhd,bkhd->bhqk', qn, k_nope)
              + jnp.einsum('bqhd,bkd->bhqk', qr, k_rope))
        p = jax.nn.softmax(sc.astype(jnp.float32) * scale, axis=-1).astype(v.dtype)
        return jnp.einsum('bhqk,bkhd->bqhd', p, v)

    qn_b = q_nope.reshape(b, nb, Q_BLOCK, h, QK_NOPE).swapaxes(0, 1)
    qr_b = q_rope.reshape(b, nb, Q_BLOCK, h, QK_ROPE).swapaxes(0, 1)
    out = lax.map(block, (qn_b, qr_b))
    return out.swapaxes(0, 1).reshape(b, s, h * V_HEAD)

def peer_ffn(u, w_q, sub_keys, peer_u, peer_v):
    b, s, d = u.shape
    ub = u.reshape((b * s) // TOK_BLOCK, TOK_BLOCK, d)

    def block(ut):
        q = (ut @ w_q).reshape(TOK_BLOCK, PEER_HEADS, 2, KEY_HALF)
        sc = jnp.einsum('thid,ind->thin', q, sub_keys).astype(jnp.float32)
        v_top, i_top = lax.top_k(sc, PEER_TOPK)
        cand = v_top[:, :, 0, :, None] + v_top[:, :, 1, None, :]
        cand_idx = i_top[:, :, 0, :, None] * N_KEYS + i_top[:, :, 1, None, :]
        cand = cand.reshape(TOK_BLOCK, PEER_HEADS, PEER_TOPK * PEER_TOPK)
        cand_idx = cand_idx.reshape(TOK_BLOCK, PEER_HEADS, PEER_TOPK * PEER_TOPK)
        best, pos = lax.top_k(cand, PEER_TOPK)
        idx = jnp.take_along_axis(cand_idx, pos, axis=-1)
        gate = jax.nn.softmax(best, axis=-1).astype(ut.dtype)
        act = jax.nn.gelu(jnp.einsum('td,thkd->thk', ut, peer_u[idx]), approximate=False)
        return jnp.einsum('thk,thkd->td', gate * act, peer_v[idx])

    return lax.map(block, ub).reshape(b, s, d)

def setup_inputs(seed: int = 0) -> dict:
    key = jax.random.key(seed)
    ks = jax.random.split(key, 32)
    f32 = jnp.float32
    nrm = lambda k, shape, scale: jax.random.normal(k, shape, f32) * scale
    gain = lambda k, n: 1.0 + 0.1 * jax.random.normal(k, (n,), f32)

    x = jax.random.normal(ks[0], (BATCH, SEQ, D_MODEL), f32)
    offsets = jax.random.randint(ks[1], (BATCH, 1), 0, 4096, dtype=jnp.int32)
    positions = offsets + jnp.arange(SEQ, dtype=jnp.int32)[None, :]

    dt_init_f = jnp.exp(jax.random.uniform(ks[6], (SSD_HEADS,), f32, math.log(1e-3), math.log(1e-1)))
    dt_init_b = jnp.exp(jax.random.uniform(ks[7], (SSD_HEADS,), f32, math.log(1e-3), math.log(1e-1)))
    inv_softplus = lambda t: t + jnp.log(-jnp.expm1(-t))

    return {
        "x": x,
        "positions": positions,
        "norm_mix_w": gain(ks[2], D_MODEL),
        "w_in": nrm(ks[3], (D_MODEL, IN_COLS), D_MODEL ** -0.5),
        "conv_w": nrm(ks[4], (CONV_WIDTH, SSD_CONV_DIM), CONV_WIDTH ** -0.5),
        "conv_b": nrm(ks[5], (SSD_CONV_DIM,), 0.02),
        "dt_bias_fwd": inv_softplus(dt_init_f),
        "dt_bias_bwd": inv_softplus(dt_init_b),
        "a_log_fwd": jnp.log(jax.random.uniform(ks[8], (SSD_HEADS,), f32, 1.0, 16.0)),
        "a_log_bwd": jnp.log(jax.random.uniform(ks[9], (SSD_HEADS,), f32, 1.0, 16.0)),
        "d_skip": gain(ks[10], SSD_HEADS),
        "ssd_norm_w": gain(ks[11], SSD_D_INNER),
        "q_a_norm_w": gain(ks[12], Q_LORA),
        "w_q_b": nrm(ks[13], (Q_LORA, MLA_HEADS * (QK_NOPE + QK_ROPE)), Q_LORA ** -0.5),
        "kv_a_norm_w": gain(ks[14], KV_LORA),
        "w_kv_b": nrm(ks[15], (KV_LORA, MLA_HEADS * (QK_NOPE + V_HEAD)), KV_LORA ** -0.5),
        "w_proj_ssd": nrm(ks[16], (SSD_D_INNER, D_MODEL), SSD_D_INNER ** -0.5),
        "w_proj_mla": nrm(ks[17], (MLA_HEADS * V_HEAD, D_MODEL), (MLA_HEADS * V_HEAD) ** -0.5),
        "w_out": nrm(ks[18], (D_MODEL, D_MODEL), D_MODEL ** -0.5),
        "norm_ffn_w": gain(ks[19], D_MODEL),
        "peer_w_q": nrm(ks[20], (D_MODEL, PEER_HEADS * 2 * KEY_HALF), D_MODEL ** -0.5),
        "peer_sub_keys": nrm(ks[21], (2, N_KEYS, KEY_HALF), KEY_HALF ** -0.5),
        "peer_u": nrm(ks[22], (N_EXPERTS, D_MODEL), D_MODEL ** -0.5),
        "peer_v": nrm(ks[23], (N_EXPERTS, D_MODEL), 0.5),
        "norm_final_w": gain(ks[24], D_MODEL),
    }

def reference(x, positions, norm_mix_w, w_in, conv_w, conv_b, dt_bias_fwd, dt_bias_bwd,
              a_log_fwd, a_log_bwd, d_skip, ssd_norm_w, q_a_norm_w, w_q_b, kv_a_norm_w,
              w_kv_b, w_proj_ssd, w_proj_mla, w_out, norm_ffn_w, peer_w_q, peer_sub_keys,
              peer_u, peer_v, norm_final_w):
    b, s, _ = x.shape
    h = x
    for _layer in range(DEPTH):
        u = rms_norm(h, norm_mix_w)
        proj = u @ w_in
        z, xbc, dt_raw, q_a, kv_a, k_rope, gate_logits = jnp.split(proj, _split_points(IN_SIZES), axis=-1)

        xbc = jax.nn.silu(depthwise_conv_centred(xbc, conv_w, conv_b))
        xs, Bm, Cm = jnp.split(xbc, [SSD_D_INNER, SSD_D_INNER + SSD_GROUPS * SSD_STATE], axis=-1)
        xh = xs.reshape(b, s, SSD_GROUPS, SSD_HPG, SSD_HEADDIM)
        Bm = Bm.reshape(b, s, SSD_GROUPS, SSD_STATE)
        Cm = Cm.reshape(b, s, SSD_GROUPS, SSD_STATE)
        dt_f_raw, dt_b_raw = jnp.split(dt_raw, 2, axis=-1)
        dt_f = jax.nn.softplus(dt_f_raw + dt_bias_fwd).reshape(b, s, SSD_GROUPS, SSD_HPG)
        dt_b = jax.nn.softplus(dt_b_raw + dt_bias_bwd).reshape(b, s, SSD_GROUPS, SSD_HPG)
        A_f = -jnp.exp(a_log_fwd).reshape(SSD_GROUPS, SSD_HPG)
        A_b = -jnp.exp(a_log_bwd).reshape(SSD_GROUPS, SSD_HPG)
        flip = lambda t: jnp.flip(t, axis=1)
        y_f = ssd_scan(xh, dt_f, A_f, Bm, Cm)
        y_b = flip(ssd_scan(flip(xh), flip(dt_b), A_b, flip(Bm), flip(Cm)))
        y = (y_f + y_b).astype(h.dtype) + xh * d_skip.reshape(SSD_GROUPS, SSD_HPG, 1)
        yg = (y.reshape(b, s, SSD_D_INNER) * jax.nn.silu(z)).reshape(b, s, SSD_GROUPS, SSD_D_INNER // SSD_GROUPS)
        y_ssd = rms_norm(yg, ssd_norm_w.reshape(SSD_GROUPS, SSD_D_INNER // SSD_GROUPS)).reshape(b, s, SSD_D_INNER)

        q = (rms_norm(q_a, q_a_norm_w) @ w_q_b).reshape(b, s, MLA_HEADS, QK_NOPE + QK_ROPE)
        q_nope, q_rope = jnp.split(q, [QK_NOPE], axis=-1)
        kv = (rms_norm(kv_a, kv_a_norm_w) @ w_kv_b).reshape(b, s, MLA_HEADS, QK_NOPE + V_HEAD)
        k_nope, v = jnp.split(kv, [QK_NOPE], axis=-1)
        cos, sin = rope_tables(positions, QK_ROPE, h.dtype)
        q_rope = apply_rope(q_rope, cos[:, :, None, :], sin[:, :, None, :])
        k_rope = apply_rope(k_rope, cos, sin)
        y_mla = mla_attention(q_nope, q_rope, k_nope, k_rope, v)

        g_ssd, g_mla = jnp.split(jax.nn.sigmoid(gate_logits), 2, axis=-1)
        m = g_ssd * (y_ssd @ w_proj_ssd) + g_mla * (y_mla @ w_proj_mla)
        h = h + m @ w_out

        h = h + peer_ffn(rms_norm(h, norm_ffn_w), peer_w_q, peer_sub_keys, peer_u, peer_v)
    return rms_norm(h, norm_final_w)


_drawn_inputs = setup_inputs


def setup_inputs(seed=0):
    import zlib

    import numpy as np

    out = dict(_drawn_inputs(seed))
    spreads = {}
    factors = {'q_a_norm_w': 3.229}
    for name, (base, spread) in spreads.items():
        noise = np.random.default_rng([zlib.crc32(name.encode()), seed]).standard_normal(out[name].shape)
        drawn = base * np.exp(spread * noise) if base else spread * noise
        out[name] = jnp.asarray(drawn.astype(out[name].dtype))
    for name, factor in factors.items():
        out[name] = (out[name] * factor).astype(out[name].dtype)
    return out
```

```python
import math

import numpy as np

import concourse.bass as bass
from concourse import mybir

F32 = mybir.dt.float32
F32R = mybir.dt.float32r
BF16 = mybir.dt.bfloat16
U32 = mybir.dt.uint32
I32 = mybir.dt.int32
ALU = mybir.AluOpType
ACT = mybir.ActivationFunctionType
AX_X = mybir.AxisListType.X

P = 128
EPS = 1e-6
CHUNK = 128
N_GROUPS = 2
HEADDIM = 64
QK_NOPE, QK_ROPE, V_HEAD = 64, 32, 64
QK = QK_NOPE + QK_ROPE
ROPE_THETA = 10000.0
TOPK = 16
NEG = -3.0e38
MASKED = -1e30
TWO_PI = 2.0 * math.pi
KB = 1024


class Ordered:

    def __init__(self, eng, sem):
        self.eng, self.sem, self.n, self.shift = eng, sem, 0, 0

    def did(self, ins):
        self.n += 1
        ins.then_inc(self.sem, 1)
        return self.n

    def wait(self, n=None):
        self.eng.wait_ge(self.sem, self.shift + (self.n if n is None else n))

    def then(self, ins):
        self.did(ins)
        self.wait()


def wait_if(eng, sem, value):
    if not isinstance(value, int) or value > 0:
        eng.wait_ge(sem, value)


def block_kernel(nc, x, positions, norm_mix_w, w_in, conv_w, conv_b, dt_bias_fwd, dt_bias_bwd,
                 a_log_fwd, a_log_bwd, d_skip, ssd_norm_w, q_a_norm_w, w_q_b, kv_a_norm_w, w_kv_b,
                 w_proj_ssd, w_proj_mla, w_out, norm_ffn_w, peer_w_q, peer_sub_keys, peer_u, peer_v,
                 norm_final_w, rope_inv, out, gates_dram, G_dram):
    _, S, D = x.shape
    TT = S // P
    KD = D // P
    D_INNER = ssd_norm_w.shape[0]
    HEADS = d_skip.shape[0]
    HPG = HEADS // N_GROUPS
    GD = D_INNER // N_GROUPS
    CONV_DIM = conv_b.shape[0]
    CT_N = CONV_DIM // P
    XS_CT = D_INNER // P
    Q_LORA, KV_LORA = q_a_norm_w.shape[0], kv_a_norm_w.shape[0]
    KQ, KKV = Q_LORA // P, KV_LORA // P
    A_HEADS = w_proj_mla.shape[0] // V_HEAD
    MID = 2 * HEADS + Q_LORA + KV_LORA + QK_ROPE
    Z0, XBC0 = 0, D_INNER
    MID0 = XBC0 + CONV_DIM
    GATE0 = MID0 + MID
    P_HEADS = peer_w_q.shape[1] // (2 * P)
    N_I = peer_u.shape[0] // P
    SCALE = float(QK) ** -0.5
    assert S == 512 and D == 1024 and P_HEADS * TOPK == P and N_I == P and CHUNK == P

    def at(name, kb, shape, dt=F32):
        return nc.alloc_sbuf_tensor_at(name, shape, dt, offset=int((17 + kb) * KB))

    ident = at("ident", 0, [P, P])
    ones = at("ones", 0.5, [P, P])
    triU = at("triU", 1, [P, P])
    triL = at("triL", 1.5, [P, P])
    iota = at("iota", 2, [P, P])
    identb = at("identb", 2.5, [P, P], BF16)
    maskF = at("maskF", 2.75, [P, P], BF16)
    maskB = at("maskB", 3, [P, P], BF16)
    vecs = at("vecs", 3.25, [P, P])
    vecT = at("vecT", 3.75, [P, P])
    dtb = at("dtb", 4.25, [P, 2 * HEADS])
    aneg = at("aneg", 4.375, [P, 2 * HEADS])
    dsk = at("dsk", 4.5, [P, HEADS])
    inv = at("inv", 4.625, [P, QK_ROPE // 2])
    posi = at("posi", 4.75, [P, TT], I32)
    posf = at("posf", 4.78125, [P, TT])
    stat = at("stat", 4.8125, [P, 64])
    trig = at("trig", 5.0625, [P, 6, TT, QK_ROPE // 2])
    sdt = at("sdt", 6.625, [P, 8, TT, 2 * HEADS])
    epsc = at("epsc", 10.75, [P, 4])
    rsum = at("rsum", 10.875, [P, 16])
    nmx = at("nmx", 10.9375, [P, 16])
    X = at("X", 12, [P, TT, D])
    actH = at("actH", 28, [P, KD, S], F32R)
    actL = at("actL", 44, [P, KD, S], F32R)
    wraw = at("wraw", 60, [P, 2, 2048])
    wH = at("wH", 76, [P, 2, 2048], F32R)
    wL = at("wL", 92, [P, 2, 2048], F32R)
    utok = at("utok", 108, [P, TT, D])
    ztok = at("ztok", 108, [P, TT, D_INNER])
    xtok = at("xtok", 124, [P, TT, D_INNER])
    BT = at("BT", 140, [P, N_GROUPS, S])
    CTt = at("CTt", 144, [P, N_GROUPS, S])
    Btok = at("Btok", 148, [P, TT, N_GROUPS * P])
    mid = at("mid", 152, [P, TT, MID])
    pre = at("pre", 163, [P, 2, S + 2])
    conv = at("conv", 167.5, [P, 2, S])
    cact = at("cact", 171.5, [P, 2, S])
    gst = at("gst", 176, [P, 2, S])
    qaH = at("qaH", 180, [P, KQ, S], F32R)
    qaL = at("qaL", 186, [P, KQ, S], F32R)
    kaH = at("kaH", 192, [P, KKV, S], F32R)
    kaL = at("kaL", 196, [P, KKV, S], F32R)
    krot = at("krot", 200, [P, TT, QK])
    kropeT = at("kropeT", 202, [P, S])
    xd = at("xd", 28, [P, 2, D_INNER])
    xdec = at("xdec", 36, [P, 2, D_INNER])
    Mx = at("Mx", 44, [P, 2, 2, 4, P])
    Lx = at("Lx", 52, [P, 2, 2, 4, P])
    prev = at("prev", 152, [P, 2, N_GROUPS, 3, GD])
    CB = at("CB", 176, [P, N_GROUPS, P])
    ya = at("ya", 36, [P, 4, GD])
    mS = at("mS", 124, [P, KD, S])
    mH = at("mH", 140, [P, KD, S], F32R)
    mL = at("mL", 156, [P, KD, S], F32R)
    mtmp = at("mtmp", 172, [P, 2, S])
    gld = at("gld", 176, [P, 2, S])
    ytok = at("ytok", 108, [P, TT, A_HEADS * V_HEAD])
    qrot = at("qrot", 140, [P, TT, 2, QK])
    rtmp = at("rtmp", 143, [P, 4, TT, 2, QK_ROPE // 2])
    QT = at("QT", 145, [P, 2, 2, S])
    KT = at("KT", 153, [P, 2, 2, S])
    Vt = at("Vt", 161, [P, 2, TT, 2, V_HEAD])
    Pr = at("Pr", 165, [P, 2, S])
    PT = at("PT", 169, [P, 2, TT, P])

    u2tok = at("u2tok", 108, [P, TT, D])
    rt = at("rt", 108, [P, 3, S])
    sc = at("sc", 124, [P, TT, 2 * P_HEADS, P])
    cur = at("cur", 156, [P, 2 * P_HEADS, P])
    pick = at("pick", 164, [P, 2 * P_HEADS, P])
    qT = at("qT", 172, [P, 2, S])
    cand = at("cand", 176, [P, P_HEADS, TOPK * TOPK])
    cand2 = at("cand2", 184, [P, P_HEADS, TOPK * TOPK])
    skraw = at("skraw", 192, [P, 2, P])
    skT = at("skT", 193, [P, 2, P])
    topv = at("topv", 194, [P, 2 * P_HEADS, TOPK])
    topi = at("topi", 195, [P, 2 * P_HEADS, TOPK], U32)
    topf = at("topf", 196, [P, 2 * P_HEADS, TOPK])
    best = at("best", 197, [P, P_HEADS, TOPK])
    bpos = at("bpos", 197.5, [P, P_HEADS, TOPK], U32)
    bab = at("bab", 198, [P, 2, P_HEADS, TOPK], U32)
    babf = at("babf", 199, [P, 2, P_HEADS, TOPK])
    gate = at("gate", 200, [P, 2, P_HEADS, TOPK])
    gsum = at("gsum", 201, [P, 2, P_HEADS])
    R3 = at("R3", 201.25, [P, 2, 3, P_HEADS * TOPK])
    TB = 32
    NTB = S // TB
    Gst = at("Gst", 60, [P, 2, N_I, TB])
    oneI = at("oneI", 92, [P, 2, 4, P])
    oneJ = at("oneJ", 96, [P, 2, 4, P])
    GRP = 4
    Uraw = at("Uraw", 60, [P, 4, D])
    Vraw = at("Vraw", 76, [P, 4, D])
    UTh = at("UTh", 92, [P, 2, KD, P], F32R)
    UTl = at("UTl", 100, [P, 2, KD, P], F32R)
    Vh = at("Vh", 108, [P, 5, D], F32R)
    Vl = at("Vl", 128, [P, 5, D], F32R)
    Wh = at("Wh", 148, [P, 5, S], F32R)
    Wl = at("Wl", 158, [P, 5, S], F32R)
    ga = at("ga", 168, [P, 2, S])
    Wf = at("Wf", 172, [P, 2, S])
    Gt = at("Gt", 176, [P, 2, NTB, GRP, TB])
    wfin = at("wfin", 192, [P, D])
    ost = at("ost", 60, [P, TT, D])

    def sem(name):
        return nc.alloc_semaphore(name)

    ps = nc.alloc_psum_tensor("ps", [P, 8, 512], F32)

    def cols(w, lo, n):
        return w.rearrange("(k p) n -> p k n", p=P)[:, :, lo:lo + n]

    kvv = w_kv_b.rearrange("(k p) n -> p k n", p=P)
    chunks = []
    for j in range(CONV_DIM // 256):
        chunks.append(("conv", j, cols(w_in, XBC0 + 256 * j, 256), KD, 256, "act"))
    MW = MID // 4
    for j in range(4):
        chunks.append(("mid", j, cols(w_in, MID0 + MW * j, MW), KD, MW, "dve"))
    for j in range(D_INNER // 256):
        chunks.append(("z", j, cols(w_in, Z0 + 256 * j, 256), KD, 256, "act"))
    for j in range(2 * D // 256):
        chunks.append(("gate", j, cols(w_in, GATE0 + 256 * j, 256), KD, 256, "act"))
    for j in range(D // 256):
        chunks.append(("pssd", j, cols(w_proj_ssd, 256 * j, 256), KD, 256, "dve"))
    for u in range(A_HEADS // 2):
        chunks.append(("q", u, cols(w_q_b, 2 * QK * u, 2 * QK), KQ, 2 * QK, "act"))
        chunks.append(("kv", u, kvv[:, :, 256 * u:256 * u + 256], KKV, 256, "dve"))
    for j in range(D // 256):
        chunks.append(("pmla", j, cols(w_proj_mla, 256 * j, 256), KD, 256, "dve"))
    for j in range(D // 256):
        chunks.append(("out", j, cols(w_out, 256 * j, 256), KD, 256, "dve"))
    for j in range(P_HEADS * 2 * P // 256):
        chunks.append(("pq", j, cols(peer_w_q, 256 * j, 256), KD, 256, "act"))
    NCH = len(chunks)
    first = {}
    for c, ch in enumerate(chunks):
        first.setdefault(ch[0], c)
    outs = {"act": 0, "dve": 0}
    taken = []
    for ch in chunks:
        outs[ch[5]] += 2
        taken.append((ch[5], outs[ch[5]]))

    def raw(c):
        _, _, _, kt, w, _ = chunks[c]
        return wraw[:, c % 2, 0:kt * w]

    def part(t, c):
        _, _, _, kt, w, _ = chunks[c]
        return t[:, c % 2, 0:kt * w]

    def part3(t, c):
        return part(t, c).rearrange("p (k n) -> p k n", k=chunks[c][3])

    small_in = sem("small_in")
    x_in = [sem(f"x_in{t}") for t in range(TT)]
    w_inq = [sem(f"w_in{s}") for s in range(2)]
    w_hi = sem("w_hi")
    w_lo = sem("w_lo")
    gemm_done = sem("gemm_done")
    v_done = sem("v_done")
    out_act = sem("out_act")
    out_dve = sem("out_dve")
    const_ready = sem("const_ready")
    vt_tr = sem("vt_tr")
    vt_ready = sem("vt_ready")
    x_sq = sem("x_sq")
    x_rt = sem("x_rt")
    u_tok = sem("u_tok")
    ts_tr = sem("ts_tr")
    ts_hi = sem("ts_hi")
    ts_lo = sem("ts_lo")
    pre_ready = sem("pre_ready")
    conv_done = sem("conv_done")
    cact_done = sem("cact_done")
    ct_tr = sem("ct_tr")
    ct_out = sem("ct_out")
    mid_done = sem("mid_done")
    mid_act = sem("mid_act")
    acs_mm = sem("acs_mm")
    a_ready = sem("a_ready")
    dvo = sem("dve_order")
    aco = sem("act_order")
    poo = sem("pool_order")
    qk_tok = sem("qk_tok")
    kr_tr = sem("kr_tr")
    kr_out = sem("kr_out")
    g_store = sem("g_store")
    g_load = [sem(f"g_load{s}") for s in range(2)]

    usedq = {}

    def chunk_used(e, c):
        if c < 0:
            return
        if chunks[c][0] == "kv":
            e.wait_ge(v_done, chunks[c][1] + 1)
        else:
            e.wait_ge(gemm_done, 2 * (c + 1))

    V_MIX, V_CW, V_CB = 0, KD, KD + 3 * CT_N
    V_SSD = V_CB + CT_N
    V_QA = V_SSD + KD
    V_KA = V_QA + KQ
    V_FFN = V_KA + KKV
    NV = V_FFN + KD
    TS = {}
    n = 0
    for name, kt in (("u", KD), ("qa", KQ), ("ka", KKV), ("ys", KD), ("ym", KD), ("u2", KD)):
        TS[name] = n
        n += kt

    def ts_bank(n):
        return 4 + n % 2

    def pe_turn(e, name, k, src):
        n = TS[name] + k
        wait_if(e, ts_lo, n - 1)
        for t in range(TT):
            ins = e.transpose(ps[:, ts_bank(n), t * P:(t + 1) * P], src(t), ident[:])
        ins.then_inc(ts_tr, 1)

    def act_turn(e, name, k, hi, col):
        n = TS[name] + k
        e.wait_ge(ts_tr, n + 1)
        scale = 1.0 if col is None else vecT[:, col + k:col + k + 1]
        e.activation(hi, ps[:, ts_bank(n), :], ACT.Copy, scale=scale).then_inc(ts_hi, 1)

    def dve_turn(e, name, k, hi, lo, col):
        n = TS[name] + k
        e.wait_ge(ts_hi, n + 1)
        scale = 1.0 if col is None else vecT[:, col + k:col + k + 1]
        e.scalar_tensor_tensor(out=lo, in0=ps[:, ts_bank(n), :], scalar=scale, in1=hi.bitcast(F32),
                               op0=ALU.mult, op1=ALU.subtract).then_inc(ts_lo, 1)

    def act_hi(e, c):
        if c >= NCH:
            return
        e.wait_ge(w_inq[c % 2], 16 * (c // 2 + 1))
        chunk_used(e, c - 2)
        e.activation(part(wH, c), raw(c), ACT.Copy).then_inc(w_hi, 1)

    def dve_lo(e, c):
        if c >= NCH:
            return
        e.wait_ge(w_hi, c + 1)
        e.tensor_tensor(part(wL, c), raw(c), part(wH, c).bitcast(F32), ALU.subtract).then_inc(w_lo, 1)

    def pe_weights(e, c):
        e.wait_ge(w_lo, c + 1)
        if c >= 2:
            who, n = taken[c - 2]
            e.wait_ge(out_act if who == "act" else out_dve, n)

    def product3(e, out_ap, pairs, first_mm=True, last_mm=True):
        n = 3 * len(pairs)
        i = 0
        for lh, ll, rh, rl in pairs:
            for a, b in ((lh, rh), (lh, rl), (ll, rh)):
                ins = e.matmul(out_ap, a, b, start=first_mm and i == 0, stop=last_mm and i == n - 1)
                i += 1
        return ins

    def pe_channels(e, c, hi, lo):
        pe_weights(e, c)
        wh, wl = part3(wH, c), part3(wL, c)
        for m in range(2):
            cs = slice(m * P, (m + 1) * P)
            product3(e, ps[:, 2 * (c % 2) + m, :],
                     [(wh[:, k, cs], wl[:, k, cs], hi[:, k, :], lo[:, k, :]) for k in range(chunks[c][3])]
                     ).then_inc(gemm_done, 1)

    def pe_tokens(e, c, hi, lo):
        pe_weights(e, c)
        wh, wl = part3(wH, c), part3(wL, c)
        w = chunks[c][4]
        for m in range(2):
            for h in range(2):
                ts = slice((2 * m + h) * P, (2 * m + h + 1) * P)
                ins = product3(e, ps[:, 2 * (c % 2) + m, h * w:(h + 1) * w],
                               [(hi[:, k, ts], lo[:, k, ts], wh[:, k, :], wl[:, k, :])
                                for k in range(chunks[c][3])])
            ins.then_inc(gemm_done, 1)

    def bank(c, m):
        return ps[:, 2 * (c % 2) + m, :]

    def bank_tokens(c, m):
        w = chunks[c][4]
        return ps[:, 2 * (c % 2) + m, 0:2 * w].rearrange("p (t n) -> p t n", t=2)


    acs_out = sem("acs_out")
    acs_exp = sem("acs_exp")
    dd_ready = sem("dd_ready")
    xdec_ready = sem("xdec_ready")
    st_mm = sem("st_mm")
    st_out = sem("st_out")
    xd_ready = sem("xd_ready")
    cb_mm = sem("cb_mm")
    cb_out = sem("cb_out")
    lr_mm = sem("lr_mm")
    lx_exp = sem("lx_exp")
    m_done = sem("m_done")
    yd_mm = sem("yd_mm")
    yo_mm = sem("yo_mm")
    ysum = sem("ysum")
    ysq = sem("ysq")
    ys_rt = sem("ys_rt")
    ys_tok = sem("ys_tok")
    g_st = [sem(f"g_st{s}") for s in range(2)]
    qrot_done = sem("qrot_done")
    kt_out = sem("kt_out")
    v_out = sem("v_out")
    q_tr = sem("q_tr")
    q_out = sem("q_out")
    s_mm = sem("s_mm")
    mx_done = sem("mx_done")
    e_done = sem("e_done")
    p_tr = sem("p_tr")
    p_out = sem("p_out")
    pv_mm = sem("pv_mm")
    y_done = sem("y_done")
    m_sum = sem("m_sum")
    m_hi = sem("m_hi")
    m_lo = sem("m_lo")

    NSC = S // CHUNK
    HD = HEADDIM

    def heads(ap):
        return ap.rearrange("p (h n) -> p h n", n=HD)

    def over(ap, n):
        return ap.unsqueeze(2).broadcast_to([ap.shape[0], ap.shape[1], n])

    attn = [(u, h, t) for u in range(A_HEADS // 2) for h in range(2) for t in range(TT)]
    NU = A_HEADS // 2

    def sp_front(e):
        for t in range(TT):
            e.dma_start(X[:, t, :], x[0, t * P:(t + 1) * P, :]).then_inc(x_in[t], 16)
        for c in range(2):
            e.dma_start(raw(c).rearrange("p (k n) -> p k n", k=chunks[c][3]), chunks[c][2]).then_inc(w_inq[c], 16)
        rows = [(norm_mix_w, V_MIX), (conv_w.rearrange("r c -> (r c)"), V_CW), (conv_b, V_CB), (ssd_norm_w, V_SSD),
                (q_a_norm_w, V_QA), (kv_a_norm_w, V_KA), (norm_ffn_w, V_FFN)]
        for v, r in rows:
            n = v.shape[0] // P
            e.dma_start(vecs[r:r + n, :], v.rearrange("(r n) -> r n", n=P)).then_inc(small_in, 16)
        for v, dst in ((dt_bias_fwd, dtb[:, 0:HEADS]), (dt_bias_bwd, dtb[:, HEADS:2 * HEADS]),
                       (a_log_fwd, aneg[:, 0:HEADS]), (a_log_bwd, aneg[:, HEADS:2 * HEADS]),
                       (d_skip, dsk[:]), (rope_inv, inv[:])):
            e.dma_start(dst, v.rearrange("(a n) -> a n", a=1).broadcast_to([P, v.shape[0]])).then_inc(small_in, 16)
        e.dma_start(posi[:], positions.rearrange("a (t p) -> p (a t)", p=P), allow_slow_non_contiguous=True).then_inc(small_in, 16)
        for c in range(2, NCH):
            e.wait_ge(w_lo, c - 1)
            e.dma_start(raw(c).rearrange("p (k n) -> p k n", k=chunks[c][3]), chunks[c][2]).then_inc(w_inq[c % 2], 16)

    SMALL = 16 * 14

    def pool_front(e):
        o = Ordered(e, poo)
        e.memset(ident[:], 0.0).then_inc(poo, 1)
        e.memset(triU[:], 0.0).then_inc(poo, 1)
        e.memset(triL[:], 0.0).then_inc(poo, 1)
        e.memset(ones[:], 1.0).then_inc(poo, 1)
        e.memset(maskF[:], 0.0).then_inc(poo, 1)
        e.memset(maskB[:], 0.0).then_inc(poo, 1)
        o.n = 6
        o.did(e.memset(epsc[:, 0:1], EPS))
        o.did(e.memset(epsc[:, 1:2], math.pi / 2))
        o.did(e.memset(pre[:], 0.0))
        o.did(e.memset(krot[:], 0.0))
        o.did(e.iota(iota[:], [[1, P]], base=0, channel_multiplier=0, allow_small_or_imprecise_dtypes=True))
        o.wait()
        def sel(t, op, fill, sign=1):
            return e.affine_select(out=t[:], in_=t[:], compare_op=op, fill=fill, base=0, pattern=[[-sign, P]],
                                   channel_multiplier=sign)
        o.did(sel(ident, ALU.not_equal, 1.0))
        o.did(sel(triU, ALU.is_gt, 1.0))
        o.did(sel(triL, ALU.is_gt, 1.0, -1))
        o.did(sel(maskF, ALU.is_ge, MASKED, -1))
        o.did(sel(maskB, ALU.is_ge, MASKED, 1))
        o.wait()
        e.tensor_copy(identb[:], ident[:]).then_inc(const_ready, 1)
        e.wait_ge(const_ready, 1)
        for i in range(2 * KD):
            e.wait_ge(out_act, taken[first["gate"] + i // 2][1] - 1 + i % 2)
            e.dma_start(gates_dram[i], gst[:, i % 2, :]).then_inc(g_st[i % 2], 16)
        for i in range(2 * KD):
            if i == 0:
                e.wait_ge(g_st[0], 16 * KD)
                e.wait_ge(g_st[1], 16 * KD)
                e.wait_ge(ysq, 2 * NSC)
                e.wait_ge(m_done, 4 * NSC)
            if i >= 2:
                c = first["pssd"] + (i - 2) // 2 if i - 2 < KD else first["pmla"] + (i - 2 - KD) // 2
                e.wait_ge(out_dve, taken[c][1] - 1 + i % 2)
            e.dma_start(gld[:, i % 2, :], gates_dram[i]).then_inc(g_load[i % 2], 16)

    def pe_front(e):
        e.wait_ge(const_ready, 1)
        e.wait_ge(small_in, SMALL)
        e.transpose(ps[:, 6, 0:NV], vecs[0:NV, :], ident[0:NV, 0:NV]).then_inc(vt_tr, 1)
        e.wait_ge(u_tok, TT)
        for k in range(KD):
            pe_turn(e, "u", k, lambda t: utok[:, t, k * P:(k + 1) * P])
        e.wait_ge(ts_lo, TS["u"] + KD)

        def turn_conv(ct):
            e.wait_ge(cact_done, ct + 1)
            wait_if(e, ct_out, ct - 1)
            src = cact[:, ct % 2, :] if ct < XS_CT else BT[:, ct - XS_CT, :]
            for t in range(TT):
                ins = e.transpose(ps[:, 4 + ct % 2, t * P:(t + 1) * P], src[:, t * P:(t + 1) * P], ident[:])
            ins.then_inc(ct_tr, 1)

        for c, (stage, j, *_) in enumerate(chunks[:first["pssd"]]):
            if stage in ("conv", "gate"):
                pe_channels(e, c, actH[:], actL[:])
            else:
                pe_tokens(e, c, actH[:], actL[:])
            if stage == "conv" and j >= 1:
                turn_conv(2 * j - 2)
                turn_conv(2 * j - 1)
            if stage == "gate" and j == 1:
                e.wait_ge(a_ready, 1)
                a = sdt[:, 1]
                e.matmul(ps[:, 6, 0:64], triU[:], a[:, :, 0:HEADS], start=True, stop=True)
                e.matmul(ps[:, 6, 64:128], triL[:], a[:, :, HEADS:2 * HEADS], start=True, stop=True)
                e.matmul(ps[:, 6, 128:256], ones[:], a[:], start=True, stop=True).then_inc(acs_mm, 1)
            if stage == "gate" and j == 3:
                e.wait_ge(ct_out, XS_CT + N_GROUPS)
                e.wait_ge(qk_tok, 2 * TT + 2)
                for t in range(TT):
                    ins = e.transpose(ps[0:QK, 7, t * P:(t + 1) * P], krot[:, t, :], ident[:])
                ins.then_inc(kr_tr, 1)
                for k in range(KQ):
                    pe_turn(e, "qa", k, lambda t: mid[:, t, 2 * HEADS + k * P:2 * HEADS + (k + 1) * P])
                for k in range(KKV):
                    pe_turn(e, "ka", k, lambda t: mid[:, t, 2 * HEADS + Q_LORA + k * P:2 * HEADS + Q_LORA + (k + 1) * P])

    def pe_ssd(e):
        for i in range(NSC - 1):
            e.wait_ge(xdec_ready, 2 * (i + 1))
            for d in range(2):
                c = i if d == 0 else NSC - 1 - i
                for g in range(N_GROUPS):
                    n = 4 * i + 2 * d + g
                    wait_if(e, st_out, n - 1)
                    if n < 2:
                        e.wait_ge(kr_out, 1)
                        e.wait_ge(acs_exp, 3)
                    e.matmul(ps[:, 6 + n % 2, :], Btok[:, c, g * P:(g + 1) * P], xdec[:, d, g * GD:(g + 1) * GD],
                             start=True, stop=True).then_inc(st_mm, 1)
        e.wait_ge(st_out, 4 * (NSC - 1))

        def rows(n):
            c, g, hf = n // 4, n // 2 % 2, n % 2
            if n == 0:
                who, cnt = taken[first["pssd"] - 1]
                e.wait_ge(out_act, cnt)
            wait_if(e, lx_exp, n - 1)
            for d in range(2):
                b = ps[:, 2 * (n % 2) + d, :]
                mask = (maskF, maskB)[d][:].unsqueeze(1).broadcast_to([P, 4, P])
                e.matmul(b.rearrange("p (h n) -> p h n", h=4), identb[:], mask, start=True, stop=False)
                for h in range(4):
                    col = d * HEADS + g * HPG + hf * 4 + h
                    ins = e.matmul(b[:, h * P:(h + 1) * P], sdt[:, 1, c, col:col + 1].broadcast_to([P, P]),
                                   (triU, triL)[d][:], start=False, stop=h == 3)
            ins.then_inc(lr_mm, 1)

        rows(0)
        for n in range(4 * NSC):
            c, g, hf = n // 4, n // 2 % 2, n % 2
            tok = slice(c * P, (c + 1) * P)
            if n % 4 == 0:
                wait_if(e, ysum, 2 * c)
                for gg in range(N_GROUPS):
                    ins = e.matmul(ps[:, 6, gg * P:(gg + 1) * P], BT[:, gg, tok], CTt[:, gg, tok], start=True, stop=True)
                ins.then_inc(cb_mm, 1)
            if n + 1 < 4 * NSC:
                rows(n + 1)
            e.wait_ge(m_done, n + 1)
            e.wait_ge(xd_ready, 2 * (c + 1))
            if n % 2 == 0:
                wait_if(e, ysum, 2 * c + g - 2 + 1)
            for h in range(4):
                hh = g * HPG + hf * 4 + h
                o = ps[:, 4 + g, (hf * 4 + h) * HD:(hf * 4 + h + 1) * HD]
                for d in range(2):
                    ins = e.matmul(o, Mx[:, n % 2, d, h, :], xd[:, d, hh * HD:(hh + 1) * HD], start=d == 0, stop=d == 1)
            ins.then_inc(yd_mm, 1)
            if hf == 1:
                wait_if(e, ysum, 2 * c + g)
                e.wait_ge(cb_out, c + 1)
                if c > 0:
                    ins = e.matmul(ps[:, 7, :], CTt[:, g, tok], prev[:, 0, g, c - 1, :], start=True, stop=True)
                if c < NSC - 1:
                    ins = e.matmul(ps[:, 6, :], CTt[:, g, tok], prev[:, 1, g, NSC - 2 - c, :], start=True, stop=True)
                ins.then_inc(yo_mm, 1)

    def pe_attention(e):
        def queries_keys(u):
            c = first["q"] + 2 * u
            if u >= 1:
                e.wait_ge(v_out, u)
                e.wait_ge(q_out, 2 * u)
            pe_tokens(e, c, qaH[:], qaL[:])
            c += 1
            pe_weights(e, c)
            wh, wl = part3(wH, c), part3(wL, c)
            for h in range(2):
                cs = slice(h * P, (h + 1) * P)
                product3(e, bank(c, h), [(wh[:, k, cs], wl[:, k, cs], kaH[:, k, :], kaL[:, k, :]) for k in range(KKV)]
                         ).then_inc(gemm_done, 1)

        def values_turn(u):
            c = first["q"] + 2 * u + 1
            wh, wl = part3(wH, c), part3(wL, c)
            e.wait_ge(out_act, taken[c - 1][1])
            for t in range(TT):
                for h in range(2):
                    vs = slice(h * P + QK_NOPE, (h + 1) * P)
                    ins = product3(e, ps[:, 0, (2 * t + h) * V_HEAD:(2 * t + h + 1) * V_HEAD],
                                   [(kaH[:, k, t * P:(t + 1) * P], kaL[:, k, t * P:(t + 1) * P], wh[:, k, vs], wl[:, k, vs])
                                    for k in range(KKV)])
            ins.then_inc(v_done, 1)
            e.wait_ge(qrot_done, 2 * (u + 1))
            for h in range(2):
                if h == 1:
                    e.wait_ge(out_dve, taken[c][1])
                for t in range(TT):
                    ins = e.transpose(ps[0:QK, 1 + h, t * P:(t + 1) * P], qrot[:, t, h, :], ident[:])
                ins.then_inc(q_tr, 1)

        def score(n):
            u, h, t = attn[n]
            wait_if(e, e_done, n - 1)
            if h == 0 and t == 0:
                e.wait_ge(q_out, 2 * (u + 1))
                e.wait_ge(out_dve, taken[first["q"] + 2 * u + 1][1])
            e.matmul(ps[:, 4 + n % 2, :], QT[0:QK, u % 2, h, t * P:(t + 1) * P], KT[0:QK, u % 2, h, :],
                     start=True, stop=True).then_inc(s_mm, 1)

        def weigh(n):
            u, h, t = attn[n]
            e.wait_ge(p_out, n + 1)
            if h == 0 and t == 0:
                e.wait_ge(v_out, u + 1)
            wait_if(e, y_done, n)
            for k in range(TT):
                ins = e.matmul(ps[:, 7, 0:V_HEAD], PT[:, n % 2, k, :],
                               Vt[:, u % 2, k, h, :], start=k == 0, stop=k == TT - 1)
            ins.then_inc(pv_mm, 1)

        e.wait_ge(ts_lo, TS["ys"] + KD)
        queries_keys(0)
        values_turn(0)
        score(0)
        for n, (u, h, t) in enumerate(attn):
            if t == 0 and u + 1 < NU:
                (queries_keys if h == 0 else values_turn)(u + 1)
            if n + 1 < len(attn):
                score(n + 1)
            e.wait_ge(e_done, n + 1)
            wait_if(e, p_out, n)
            for k in range(TT):
                ins = e.transpose(ps[:, 6, k * P:(k + 1) * P], Pr[:, n % 2, k * P:(k + 1) * P], ident[:])
            ins.then_inc(p_tr, 1)
            if n >= 1:
                weigh(n - 1)
        weigh(len(attn) - 1)

    def pe_merge(e):
        e.wait_ge(y_done, len(attn))
        for k in range(KD):
            pe_turn(e, "ym", k, lambda t: ytok[:, t, k * P:(k + 1) * P])
        e.wait_ge(ts_lo, TS["ym"] + KD)
        for c in range(first["pmla"], first["out"]):
            pe_channels(e, c, actH[:], actL[:])
        e.wait_ge(m_lo, KD)
        for c in range(first["out"], first["pq"]):
            pe_tokens(e, c, mH[:], mL[:])

    def act_front(e, o):
        for t in range(TT):
            e.wait_ge(x_in[t], 16)
            e.activation(utok[:, t, :], X[:, t, :], ACT.Square, accum_out=stat[:, t:t + 1]).then_inc(x_sq, 1)
        e.wait_ge(x_sq, TT)
        e.wait_ge(const_ready, 1)
        e.activation(stat[:, 4:8], stat[:, 0:4], ACT.Sqrt, bias=epsc[:, 0:1], scale=1.0 / D).then_inc(x_rt, 1)
        e.wait_ge(small_in, SMALL)
        e.activation(sdt[:, 6, 0, :], aneg[:], ACT.Exp).then_inc(mid_act, 1)
        act_hi(e, 0)
        e.wait_ge(vt_ready, 1)
        for k in range(KD):
            act_turn(e, "u", k, actH[:, k, :], V_MIX)

        def silu_conv(ct):
            e.wait_ge(conv_done, ct + 1)
            wait_if(e, ct_tr, ct - 1 if ct < XS_CT else 0)
            dst = cact[:, ct % 2, :] if ct < XS_CT else BT[:, ct - XS_CT, :] if ct < XS_CT + N_GROUPS \
                else CTt[:, ct - XS_CT - N_GROUPS, :]
            e.activation(dst, conv[:, ct % 2, :], ACT.Silu).then_inc(cact_done, 1)

        for c, (stage, j, *_) in enumerate(chunks[:first["pssd"]]):
            act_hi(e, c + 1)
            if stage == "conv":
                for m in range(2):
                    ct = 2 * j + m
                    e.wait_ge(gemm_done, 2 * c + m + 1)
                    wait_if(e, conv_done, ct - 1)
                    e.activation(pre[:, m, 1:S + 1], bank(c, m), ACT.Copy).then_inc(out_act, 1)
                    if ct >= 1:
                        silu_conv(ct - 1)
            if stage == "mid" and j == 0:
                silu_conv(CT_N - 1)
            if stage == "z":
                for m in range(2):
                    e.wait_ge(gemm_done, 2 * c + m + 1)
                    e.activation(ztok[:, 2 * m:2 * m + 2, j * 256:(j + 1) * 256], bank_tokens(c, m), ACT.Silu
                                 ).then_inc(out_act, 1)
            if stage == "z" and j == 3:
                e.wait_ge(mid_done, 1)
                e.activation(sdt[:, 7], sdt[:, 6], ACT.Exp, scale=-1.0).then_inc(mid_act, 1)
                e.wait_ge(mid_done, 2)
                e.activation(sdt[:, 4], sdt[:, 2], ACT.Ln).then_inc(mid_act, 1)
                e.wait_ge(mid_done, 3)
                e.activation(trig[:, 0], trig[:, 2], ACT.Sin)
                e.activation(trig[:, 1], trig[:, 3], ACT.Sin, bias=epsc[:, 1:2], scale=-1.0).then_inc(mid_act, 1)
                e.wait_ge(out_dve, taken[first["mid"] + 3][1])
                for t in range(TT):
                    o.then(e.activation(gst[:, 0, 0:Q_LORA], mid[:, t, 2 * HEADS:2 * HEADS + Q_LORA], ACT.Square,
                                        accum_out=stat[:, 12 + t:13 + t]))
                    o.then(e.activation(gst[:, 1, 0:KV_LORA], mid[:, t, 2 * HEADS + Q_LORA:2 * HEADS + Q_LORA + KV_LORA],
                                        ACT.Square, accum_out=stat[:, 16 + t:17 + t]))
                o.did(e.activation(stat[:, 20:24], stat[:, 12:16], ACT.Sqrt, bias=epsc[:, 0:1], scale=1.0 / Q_LORA))
                e.activation(stat[:, 24:28], stat[:, 16:20], ACT.Sqrt, bias=epsc[:, 0:1], scale=1.0 / KV_LORA
                             ).then_inc(mid_act, 1)
            if stage == "gate":
                for m in range(2):
                    e.wait_ge(gemm_done, 2 * c + m + 1)
                    wait_if(e, g_st[m], 16 * j)
                    e.activation(gst[:, m, :], bank(c, m), ACT.Sigmoid).then_inc(out_act, 1)
            if stage == "gate" and j == 2:
                e.wait_ge(acs_out, 2)
                e.activation(sdt[:, 4], sdt[:, 2], ACT.Exp).then_inc(acs_exp, 1)
                e.activation(sdt[:, 6], sdt[:, 5], ACT.Exp).then_inc(acs_exp, 1)
                e.activation(sdt[:, 7], ps[:, 6, 128:256].rearrange("p (t h) -> p t h", t=TT), ACT.Exp
                             ).then_inc(acs_exp, 1)
            if stage == "gate" and j == 3:
                for k in range(KQ):
                    act_turn(e, "qa", k, qaH[:, k, :], V_QA)
                for k in range(KKV):
                    act_turn(e, "ka", k, kaH[:, k, :], V_KA)

    def act_ssd(e):
        for n in range(4 * NSC):
            c, g, hf = n // 4, n // 2 % 2, n % 2
            e.wait_ge(lr_mm, n + 1)
            wait_if(e, m_done, n - 1)
            for d in range(2):
                for h in range(4):
                    col = d * HEADS + g * HPG + hf * 4 + h
                    ins = e.activation(Lx[:, n % 2, d, h, :], ps[:, 2 * (n % 2) + d, h * P:(h + 1) * P], ACT.Exp,
                                       bias=sdt[:, 3, c, col:col + 1])
            ins.then_inc(lx_exp, 1)
            if n % 2 == 1 and n >= 3:
                square_y(e, (n - 3) // 2)
        square_y(e, 2 * NSC - 1)
        e.wait_ge(ysq, 2 * NSC)
        e.activation(stat[:, 44:52], stat[:, 36:44], ACT.Sqrt, bias=epsc[:, 0:1], scale=1.0 / GD).then_inc(ys_rt, 1)

    def square_y(e, i):
        c, g = i // 2, i % 2
        e.wait_ge(ysum, i + 1)
        wait_if(e, ysq, i)
        e.activation(ya[:, 3, :], ztok[:, c, g * GD:(g + 1) * GD], ACT.Square,
                     accum_out=stat[:, 36 + i:37 + i]).then_inc(ysq, 1)

    def act_pssd(e):
        for k in range(KD):
            act_turn(e, "ys", k, actH[:, k, :], V_SSD)
        for c in range(first["pssd"], first["q"]):
            act_hi(e, c + 1)

    def act_attention(e):
        def queries_out(u):
            c = first["q"] + 2 * u
            if u == 0:
                act_hi(e, c + 1)
            for m in range(2):
                e.wait_ge(gemm_done, 2 * c + m + 1)
                if u >= 1:
                    e.wait_ge(q_tr, 2 * u)
                e.activation(qrot[:, 2 * m:2 * m + 2, :, :], bank_tokens(c, m).rearrange("p t (h n) -> p t h n", h=2),
                             ACT.Copy, scale=SCALE).then_inc(out_act, 1)

        def rest_out(u):
            c = first["q"] + 2 * u + 1
            for h in range(2):
                e.wait_ge(q_tr, 2 * u + h + 1)
                if u >= 2:
                    e.wait_ge(s_mm, 8 * (u - 1))
                e.activation(QT[0:QK, u % 2, h, :], ps[0:QK, 1 + h, :], ACT.Copy).then_inc(q_out, 1)
            act_hi(e, c + 1)
            act_hi(e, c + 2)

        queries_out(0)
        rest_out(0)
        for n, (u, h, t) in enumerate(attn):
            if t == 2 and h == 0 and u + 1 < NU:
                queries_out(u + 1)
            if t == 1 and h == 1 and u + 1 < NU:
                rest_out(u + 1)
            e.wait_ge(mx_done, n + 1)
            wait_if(e, p_tr, n - 1)
            e.activation(Pr[:, n % 2, :], ps[:, 4 + n % 2, :], ACT.Exp, bias=nmx[:, n % 4:n % 4 + 1],
                         accum_out=rsum[:, n % 4:n % 4 + 1]).then_inc(e_done, 1)
            if n >= 1:
                copy_p(e, n - 1)
        copy_p(e, len(attn) - 1)

    def copy_p(e, n):
        e.wait_ge(p_tr, n + 1)
        wait_if(e, pv_mm, n - 1)
        e.activation(PT[:, n % 2, :, :], ps[:, 6, :].rearrange("p (k n) -> p k n", k=TT), ACT.Copy).then_inc(p_out, 1)

    def act_merge(e):
        for k in range(KD):
            act_turn(e, "ym", k, actH[:, k, :], None)
        for c in range(first["pmla"], first["out"]):
            if c > first["pmla"]:
                act_hi(e, c + 1)
            for m in range(2):
                i = 2 * (c - first["pmla"]) + m
                e.wait_ge(m_sum, i + 1)
                e.activation(mH[:, i, :], mtmp[:, i % 2, :], ACT.Copy).then_inc(m_hi, 1)
        for c in range(first["out"], first["pq"]):
            act_hi(e, c + 1)

    def dve_front(e, o):
        e.wait_ge(x_rt, 1)
        o.then(e.reciprocal(stat[:, 8:12], stat[:, 4:8]))
        for t in range(TT):
            e.tensor_scalar(utok[:, t, :], X[:, t, :], stat[:, 8 + t:9 + t], None, ALU.mult).then_inc(u_tok, 1)
        e.wait_ge(vt_tr, 1)
        e.tensor_copy(vecT[:, 0:NV], ps[:, 6, 0:NV]).then_inc(vt_ready, 1)
        e.wait_ge(mid_act, 1)
        o.did(e.tensor_scalar(aneg[:], sdt[:, 6, 0, :], -1.0, None, ALU.mult))
        o.then(e.tensor_copy(posf[:], posi[:]))
        NF = QK_ROPE // 2
        o.then(e.tensor_tensor(trig[:, 2], posf[:].unsqueeze(2).broadcast_to([P, TT, NF]),
                               inv[:].unsqueeze(1).broadcast_to([P, TT, NF]), ALU.mult))
        big = 1.5 * 2 ** 23
        o.then(e.tensor_scalar(trig[:, 3], trig[:, 2], 1.0 / TWO_PI, big, ALU.mult, ALU.add))
        o.then(e.tensor_scalar(trig[:, 3], trig[:, 3], -big, None, ALU.add))
        c1 = 6.28125
        c2 = float(np.round((TWO_PI - c1) * 2 ** 20) / 2 ** 20)
        c3 = TWO_PI - c1 - c2
        for cc in (c1, c2, c3):
            o.then(e.scalar_tensor_tensor(out=trig[:, 2], in0=trig[:, 3], scalar=-cc, in1=trig[:, 2],
                                          op0=ALU.mult, op1=ALU.add))
        o.then(e.tensor_scalar(trig[:, 2], trig[:, 2], 3.1415925, -3.1415925, ALU.min, ALU.max))
        o.did(e.scalar_tensor_tensor(out=trig[:, 3], in0=trig[:, 2], scalar=-1.0, in1=trig[:, 2], op0=ALU.mult, op1=ALU.max))
        dve_lo(e, 0)
        for k in range(KD):
            dve_turn(e, "u", k, actH[:, k, :], actL[:, k, :], V_MIX)

        def conv_out(ct):
            e.wait_ge(ct_tr, ct + 1)
            dst = xtok[:, :, ct * P:(ct + 1) * P] if ct < XS_CT else Btok[:, :, (ct - XS_CT) * P:(ct - XS_CT + 1) * P]
            e.tensor_copy(dst, ps[:, 4 + ct % 2, :].rearrange("p (t n) -> p t n", t=TT)).then_inc(ct_out, 1)

        for c, (stage, j, *_) in enumerate(chunks[:first["pssd"]]):
            dve_lo(e, c + 1)
            if stage == "conv":
                for m in range(2):
                    ct = 2 * j + m
                    e.wait_ge(out_act, 2 * c + m + 1)
                    wait_if(e, cact_done, ct - 1)
                    w = [vecT[:, V_CW + CT_N * r + ct:V_CW + CT_N * r + ct + 1] for r in range(3)]
                    bias = vecT[:, V_CB + ct:V_CB + ct + 1]
                    o.then(e.tensor_scalar(conv[:, m, :], pre[:, m, 0:S], w[0], bias, ALU.mult, ALU.add))
                    o.then(e.scalar_tensor_tensor(out=conv[:, m, :], in0=pre[:, m, 1:S + 1], scalar=w[1],
                                                  in1=conv[:, m, :], op0=ALU.mult, op1=ALU.add))
                    e.scalar_tensor_tensor(out=conv[:, m, :], in0=pre[:, m, 2:S + 2], scalar=w[2],
                                           in1=conv[:, m, :], op0=ALU.mult, op1=ALU.add).then_inc(conv_done, 1)
                if j >= 1:
                    conv_out(2 * j - 2)
                    conv_out(2 * j - 1)
            if stage == "mid":
                for m in range(2):
                    e.wait_ge(gemm_done, 2 * c + m + 1)
                    e.tensor_copy(mid[:, 2 * m:2 * m + 2, j * MW:(j + 1) * MW], bank_tokens(c, m)).then_inc(out_dve, 1)
            if stage == "mid" and j == 3:
                e.wait_ge(out_dve, taken[c][1])
                o.then(e.tensor_tensor(sdt[:, 5], mid[:, :, 0:2 * HEADS],
                                       dtb[:].unsqueeze(1).broadcast_to([P, TT, 2 * HEADS]), ALU.add))
                e.scalar_tensor_tensor(out=sdt[:, 6], in0=sdt[:, 5], scalar=-1.0, in1=sdt[:, 5], op0=ALU.mult, op1=ALU.max).then_inc(mid_done, 1)
            if stage == "z" and j == 3:
                e.wait_ge(mid_act, 2)
                e.tensor_scalar(sdt[:, 2], sdt[:, 7], 1.0, None, ALU.add).then_inc(mid_done, 1)
                e.wait_ge(dvo, o.n)
                e.wait_ge(mid_done, 2)
                o.then(e.tensor_scalar(sdt[:, 3], sdt[:, 2], -1.0, 1e-37, ALU.add, ALU.max))
                e.reciprocal(sdt[:, 3], sdt[:, 3]).then_inc(mid_done, 1)
                e.wait_ge(mid_done, 3)
                e.wait_ge(mid_act, 3)
                o.then(e.tensor_tensor(sdt[:, 6], sdt[:, 4], sdt[:, 7], ALU.mult))
                o.then(e.tensor_tensor(sdt[:, 6], sdt[:, 6], sdt[:, 3], ALU.mult))
                o.then(e.scalar_tensor_tensor(out=sdt[:, 0], in0=sdt[:, 5], scalar=0.0, in1=sdt[:, 6],
                                              op0=ALU.max, op1=ALU.add))
                e.tensor_tensor(sdt[:, 1], sdt[:, 0], aneg[:].unsqueeze(1).broadcast_to([P, TT, 2 * HEADS]),
                                ALU.mult).then_inc(a_ready, 1)
            if stage == "gate" and j == 0:
                e.wait_ge(mid_act, 5)
                o.then(e.reciprocal(stat[:, 28:36], stat[:, 20:28]))
                for t in range(TT):
                    q0 = 2 * HEADS
                    e.tensor_scalar(mid[:, t, q0:q0 + Q_LORA], mid[:, t, q0:q0 + Q_LORA], stat[:, 28 + t:29 + t],
                                    None, ALU.mult).then_inc(qk_tok, 1)
                    q0 += Q_LORA
                    e.tensor_scalar(mid[:, t, q0:q0 + KV_LORA], mid[:, t, q0:q0 + KV_LORA], stat[:, 32 + t:33 + t],
                                    None, ALU.mult).then_inc(qk_tok, 1)
                r0 = MID - QK_ROPE
                x1, x2 = mid[:, :, r0:r0 + NF], mid[:, :, r0 + NF:r0 + 2 * NF]
                o.did(e.tensor_tensor(trig[:, 2], x1, trig[:, 1], ALU.mult))
                o.did(e.tensor_tensor(trig[:, 3], x2, trig[:, 0], ALU.mult))
                o.did(e.tensor_tensor(trig[:, 4], x1, trig[:, 0], ALU.mult))
                o.then(e.tensor_tensor(trig[:, 5], x2, trig[:, 1], ALU.mult))
                e.tensor_tensor(krot[:, :, QK_NOPE:QK_NOPE + NF], trig[:, 2], trig[:, 3], ALU.subtract).then_inc(qk_tok, 1)
                e.tensor_tensor(krot[:, :, QK_NOPE + NF:QK], trig[:, 4], trig[:, 5], ALU.add).then_inc(qk_tok, 1)
            if stage == "gate" and j == 2:
                e.wait_ge(acs_mm, 1)
                o.did(e.tensor_copy(sdt[:, 2, :, 0:HEADS], ps[:, 6, 0:64].rearrange("p (t h) -> p t h", t=TT)))
                o.then(e.tensor_copy(sdt[:, 2, :, HEADS:2 * HEADS], ps[:, 6, 64:128].rearrange("p (t h) -> p t h", t=TT)))
                e.tensor_scalar(sdt[:, 3], sdt[:, 2], -1.0, None, ALU.mult).then_inc(acs_out, 1)
                e.tensor_tensor(sdt[:, 5], ps[:, 6, 128:256].rearrange("p (t h) -> p t h", t=TT), sdt[:, 2],
                                ALU.subtract).then_inc(acs_out, 1)
            if stage == "gate" and j == 3:
                e.wait_ge(acs_exp, 3)
                o.then(e.tensor_tensor(sdt[:, 5], sdt[:, 0], sdt[:, 6], ALU.mult))
            if stage == "gate" and j == 3:
                e.wait_ge(kr_tr, 1)
                e.tensor_copy(kropeT[QK_NOPE:QK, :], ps[QK_NOPE:QK, 7, :]).then_inc(kr_out, 1)
                for k in range(KQ):
                    dve_turn(e, "qa", k, qaH[:, k, :], qaL[:, k, :], V_QA)
                for k in range(KKV):
                    dve_turn(e, "ka", k, kaH[:, k, :], kaL[:, k, :], V_KA)

    def dve_ssd(e, o):
        e.wait_ge(gemm_done, 2 * first["pssd"])

        def fac(k, c, d):
            return over(sdt[:, k, c, d * HEADS:(d + 1) * HEADS], HD)

        for i in range(NSC - 1):
            wait_if(e, st_mm, 4 * i)
            for d in range(2):
                c = i if d == 0 else NSC - 1 - i
                e.tensor_tensor(heads(xdec[:, d, :]), heads(xtok[:, c, :]), fac(5, c, d), ALU.mult).then_inc(xdec_ready, 1)
            for d in range(2):
                c = i if d == 0 else NSC - 1 - i
                for g in range(N_GROUPS):
                    n = 4 * i + 2 * d + g
                    dst = prev[:, d, g, i, :]
                    if i == 0:
                        if n == 0:
                            e.wait_ge(ts_tr, TS["ka"] + KKV)
                        e.wait_ge(st_mm, n + 1)
                        e.tensor_copy(dst, ps[:, 6 + n % 2, :]).then_inc(st_out, 1)
                        continue
                    e.wait_ge(st_out, 4 * i)
                    dec = over(sdt[:, 7, c, d * HEADS + g * HPG:d * HEADS + (g + 1) * HPG], HD)
                    o.then(e.tensor_tensor(heads(dst), heads(prev[:, d, g, i - 1, :]), dec, ALU.mult))
                    e.wait_ge(st_mm, n + 1)
                    e.tensor_tensor(dst, ps[:, 6 + n % 2, :], dst, ALU.add).then_inc(st_out, 1)
        e.wait_ge(g_st[0], 16 * KD)
        e.wait_ge(g_st[1], 16 * KD)
        for n in range(4 * NSC):
            c, g, hf = n // 4, n // 2 % 2, n % 2
            if n % 4 == 0:
                wait_if(e, yd_mm, n)
                for d in range(2):
                    e.tensor_tensor(heads(xd[:, d, :]), heads(xtok[:, c, :]), fac(0, c, d), ALU.mult).then_inc(xd_ready, 1)
                e.wait_ge(cb_mm, c + 1)
                e.tensor_copy(CB[:], ps[:, 6, 0:N_GROUPS * P].rearrange("p (g n) -> p g n", g=N_GROUPS)).then_inc(cb_out, 1)
                e.wait_ge(cb_out, c + 1)
            e.wait_ge(lx_exp, n + 1)
            wait_if(e, yd_mm, n - 1)
            e.tensor_tensor(Mx[:, n % 2].rearrange("p d h n -> p (d h) n"), Lx[:, n % 2].rearrange("p d h n -> p (d h) n"),
                            CB[:, g, :].unsqueeze(1).broadcast_to([P, 8, P]), ALU.mult).then_inc(m_done, 1)
            if hf == 1:
                gs = slice(g * GD, (g + 1) * GD)
                hs = slice(g * HPG, (g + 1) * HPG)
                o.did(e.tensor_tensor(heads(ya[:, 0, :]), heads(xtok[:, c, gs]), over(dsk[:, hs], HD), ALU.mult))
                e.wait_ge(yo_mm, 2 * c + g + 1)
                if c > 0:
                    o.did(e.tensor_tensor(heads(ya[:, 1, :]), heads(ps[:, 7, :]), over(sdt[:, 4, c, hs], HD), ALU.mult))
                if c < NSC - 1:
                    o.did(e.tensor_tensor(heads(ya[:, 2, :]), heads(ps[:, 6, :]),
                                          over(sdt[:, 4, c, HEADS + g * HPG:HEADS + (g + 1) * HPG], HD), ALU.mult))
                o.wait()
                o.then(e.tensor_tensor(ya[:, 0, :], ps[:, 4 + g, :], ya[:, 0, :], ALU.add))
                if c > 0:
                    o.then(e.tensor_tensor(ya[:, 0, :], ya[:, 0, :], ya[:, 1, :], ALU.add))
                if c < NSC - 1:
                    o.then(e.tensor_tensor(ya[:, 0, :], ya[:, 0, :], ya[:, 2, :], ALU.add))
                e.tensor_tensor(ztok[:, c, gs], ya[:, 0, :], ztok[:, c, gs], ALU.mult).then_inc(ysum, 1)
                e.wait_ge(ysum, 2 * c + g + 1)
        e.wait_ge(ys_rt, 1)
        o.then(e.reciprocal(stat[:, 52:60], stat[:, 44:52]))
        for i in range(2 * NSC):
            c, g = i // 2, i % 2
            gs = slice(g * GD, (g + 1) * GD)
            e.tensor_scalar(ztok[:, c, gs], ztok[:, c, gs], stat[:, 52 + i:53 + i], None, ALU.mult).then_inc(ys_tok, 1)

    def gated(e, c, m, base):
        i = base + 2 * (c - first["pssd" if base == 0 else "pmla"]) + m
        e.wait_ge(g_load[i % 2], 16 * (i // 2 + 1))
        e.wait_ge(gemm_done, 2 * c + m + 1)
        return i

    def dve_pssd(e):
        for k in range(KD):
            dve_turn(e, "ys", k, actH[:, k, :], actL[:, k, :], V_SSD)
        for c in range(first["pssd"], first["q"]):
            dve_lo(e, c + 1)
            for m in range(2):
                i = gated(e, c, m, 0)
                e.tensor_tensor(mS[:, i, :], bank(c, m), gld[:, i % 2, :], ALU.mult).then_inc(out_dve, 1)

    def dve_attention(e, o):
        NF = QK_ROPE // 2
        for s in range(2):
            for h in range(2):
                o.did(e.tensor_copy(KT[QK_NOPE:QK, s, h, :], kropeT[QK_NOPE:QK, :]))
        o.wait()

        def rotate(u):
            c = first["q"] + 2 * u
            if u == 0:
                dve_lo(e, c + 1)
            e.wait_ge(out_act, taken[c][1])
            x1 = qrot[:, :, :, QK_NOPE:QK_NOPE + NF]
            x2 = qrot[:, :, :, QK_NOPE + NF:QK]
            sin = trig[:, 0].unsqueeze(2).broadcast_to([P, TT, 2, NF])
            cos = trig[:, 1].unsqueeze(2).broadcast_to([P, TT, 2, NF])
            o.did(e.tensor_tensor(rtmp[:, 0], x1, cos, ALU.mult))
            o.did(e.tensor_tensor(rtmp[:, 1], x2, sin, ALU.mult))
            o.did(e.tensor_tensor(rtmp[:, 2], x1, sin, ALU.mult))
            o.then(e.tensor_tensor(rtmp[:, 3], x2, cos, ALU.mult))
            e.tensor_tensor(x1, rtmp[:, 0], rtmp[:, 1], ALU.subtract).then_inc(qrot_done, 1)
            e.tensor_tensor(x2, rtmp[:, 2], rtmp[:, 3], ALU.add).then_inc(qrot_done, 1)
            c += 1
            for h in range(2):
                e.wait_ge(gemm_done, 2 * c + h + 1)
                if u >= 2:
                    e.wait_ge(s_mm, 8 * (u - 1))
                e.tensor_copy(KT[0:QK_NOPE, u % 2, h, :], ps[0:QK_NOPE, 2 * (c % 2) + h, :]).then_inc(out_dve, 1)

        def values_out(u):
            c = first["q"] + 2 * u + 1
            e.wait_ge(v_done, u + 1)
            if u >= 2:
                e.wait_ge(pv_mm, 8 * (u - 1))
            e.tensor_copy(Vt[:, u % 2].rearrange("p t h n -> p (t h n)"), ps[:, 0, :]).then_inc(v_out, 1)
            dve_lo(e, c + 1)
            dve_lo(e, c + 2)

        def row_max(n):
            e.wait_ge(s_mm, n + 1)
            wait_if(e, e_done, n - 3)
            e.tensor_reduce(nmx[:, n % 4:n % 4 + 1], ps[:, 4 + n % 2, :], AX_X, ALU.max, negate=True).then_inc(mx_done, 1)

        rotate(0)
        values_out(0)
        row_max(0)
        for n, (u, h, t) in enumerate(attn):
            if n + 1 < len(attn):
                row_max(n + 1)
            if t == 2 and h == 0 and u + 1 < NU:
                rotate(u + 1)
            if t == 1 and h == 1 and u + 1 < NU:
                values_out(u + 1)
            e.wait_ge(e_done, n + 1)
            o.then(e.reciprocal(rsum[:, 8 + n % 4:9 + n % 4], rsum[:, n % 4:n % 4 + 1]))
            e.wait_ge(pv_mm, n + 1)
            hd = (2 * u + h) * V_HEAD
            e.tensor_scalar(ytok[:, t, hd:hd + V_HEAD], ps[:, 7, 0:V_HEAD],
                            rsum[:, 8 + n % 4:9 + n % 4], None, ALU.mult).then_inc(y_done, 1)

    def dve_merge(e):
        for k in range(KD):
            dve_turn(e, "ym", k, actH[:, k, :], actL[:, k, :], None)
        for c in range(first["pmla"], first["out"]):
            if c > first["pmla"]:
                dve_lo(e, c + 1)
            for m in range(2):
                i = gated(e, c, m, KD)
                ct = i - KD
                wait_if(e, m_lo, ct - 1)
                e.tensor_tensor(mtmp[:, i % 2, :], bank(c, m), gld[:, i % 2, :], ALU.mult).then_inc(out_dve, 1)
                e.wait_ge(out_dve, taken[c][1] - 1 + m)
                e.tensor_tensor(mtmp[:, i % 2, :], mtmp[:, i % 2, :], mS[:, ct, :], ALU.add).then_inc(m_sum, 1)
                e.wait_ge(m_hi, ct + 1)
                e.tensor_tensor(mL[:, ct, :], mtmp[:, i % 2, :], mH[:, ct, :].bitcast(F32), ALU.subtract).then_inc(m_lo, 1)
        for c in range(first["out"], first["pq"]):
            dve_lo(e, c + 1)
            j = c - first["out"]
            for m in range(2):
                e.wait_ge(gemm_done, 2 * c + m + 1)
                dst = X[:, 2 * m:2 * m + 2, j * 256:(j + 1) * 256]
                e.tensor_tensor(dst, bank_tokens(c, m), dst, ALU.add).then_inc(out_dve, 1)


    h_sq, h_rt = sem("h_sq"), sem("h_rt")
    u2_tok = sem("u2_tok")
    sk_in, sk_tr, sk_out = sem("sk_in"), sem("sk_tr"), sem("sk_out")
    sc_mm = sem("sc_mm")
    sc_out = sem("sc_out")
    g_shift, g_exp = sem("g_shift"), sem("g_exp")
    r_done, r_tr, r_out = sem("r_done"), sem("r_tr"), sem("r_out")
    oh_done = sem("oh_done")
    gq_mm = sem("gq_mm")
    gq_out = sem("gq_out")
    gb_st = [sem(f"gb_st{s}") for s in range(2)]
    u_in = [sem(f"u_in{s}") for s in range(4)]
    v_in = [sem(f"v_in{s}") for s in range(4)]
    gt_in = [sem(f"gt_in{s}") for s in range(2)]
    wf_in = sem("wf_in")
    t_mm = sem("t_mm")
    t_hi = sem("t_hi")
    t_lo = sem("t_lo")
    h_mm = sem("h_mm")
    h_gelu = sem("h_gelu")
    w_mul = sem("w_mul")
    wt_hi = sem("wt_hi")
    wt_lo = sem("wt_lo")
    vt_hi = sem("vt_hi")
    vt_lo = sem("vt_lo")
    o_mm = sem("o_mm")
    o_add = sem("o_add")
    f_sq, f_rt, f_out, f_st = sem("f_sq"), sem("f_rt"), sem("f_out"), sem("f_st")

    NPQ = first["pq"]
    E_TILES = peer_u.shape[0] // P
    NITER = E_TILES // (2 * GRP)
    QPB = TB // 4

    def pe_routing(e):
        e.wait_ge(u2_tok, TT)
        for k in range(KD):
            pe_turn(e, "u2", k, lambda t: u2tok[:, t, k * P:(k + 1) * P])
        e.wait_ge(sk_in, 16)
        for i in range(2):
            ins = e.transpose(ps[:, 6, i * P:(i + 1) * P], skraw[:, i, :], ident[:])
        ins.then_inc(sk_tr, 1)
        e.wait_ge(ts_lo, TS["u2"] + KD)

        def scores(c, m):
            s = 2 * (c - NPQ) + m
            e.wait_ge(out_act, taken[c][1] - 1 + m)
            wait_if(e, sc_out, s - 1)
            for t in range(TT):
                ins = e.matmul(ps[:, 4 + s % 2, t * P:(t + 1) * P], qT[:, m, t * P:(t + 1) * P], skT[:, s % 2, :],
                               start=True, stop=True)
            ins.then_inc(sc_mm, 1)

        e.wait_ge(sk_out, 1)
        for c in range(NPQ, NCH):
            pe_channels(e, c, actH[:], actL[:])
            if c > NPQ:
                scores(c - 1, 0)
                scores(c - 1, 1)
        scores(NCH - 1, 0)
        scores(NCH - 1, 1)
        for t in range(TT):
            e.wait_ge(r_done, 3 * (t + 1))
            wait_if(e, r_out, t)
            for r in range(3):
                ins = e.transpose(ps[:, 6, r * P:(r + 1) * P], R3[:, t % 2, r, :], ident[:])
            ins.then_inc(r_tr, 1)

    def act_routing(e):
        for t in range(TT):
            e.wait_ge(out_dve, taken[NPQ - 1][1])
            wait_if(e, h_sq, t)
            if t == 0:
                e.wait_ge(ts_tr, TS["ym"] + KD)
            e.activation(u2tok[:, t, :], X[:, t, :], ACT.Square, accum_out=stat[:, t:t + 1]).then_inc(h_sq, 1)
        e.wait_ge(h_sq, TT)
        e.activation(stat[:, 4:8], stat[:, 0:4], ACT.Sqrt, bias=epsc[:, 0:1], scale=1.0 / D).then_inc(h_rt, 1)
        for k in range(KD):
            act_turn(e, "u2", k, actH[:, k, :], V_FFN)
        for c in range(NPQ, NCH):
            act_hi(e, c + 1)
            for m in range(2):
                e.wait_ge(gemm_done, 2 * c + m + 1)
                if c > NPQ:
                    e.wait_ge(sc_mm, 2 * (c - NPQ) + m - 1)
                e.activation(qT[:, m, :], bank(c, m), ACT.Copy).then_inc(out_act, 1)
        for t in range(TT):
            e.wait_ge(g_shift, t + 1)
            e.activation(gate[:, 1], gate[:, 0], ACT.Exp).then_inc(g_exp, 1)

    def dve_routing(e, o):
        e.wait_ge(h_rt, 1)
        o.then(e.reciprocal(stat[:, 8:12], stat[:, 4:8]))
        for t in range(TT):
            e.tensor_scalar(u2tok[:, t, :], X[:, t, :], stat[:, 8 + t:9 + t], None, ALU.mult).then_inc(u2_tok, 1)
        for k in range(KD):
            dve_turn(e, "u2", k, actH[:, k, :], actL[:, k, :], V_FFN)
        e.wait_ge(sk_tr, 1)
        e.tensor_copy(skT[:].rearrange("p i n -> p (i n)"), ps[:, 6, 0:2 * P]).then_inc(sk_out, 1)

        def scores_out(s):
            e.wait_ge(sc_mm, s + 1)
            e.tensor_copy(sc[:, :, s, :], ps[:, 4 + s % 2, :].rearrange("p (t n) -> p t n", t=TT)).then_inc(sc_out, 1)

        for c in range(NPQ, NCH):
            dve_lo(e, c + 1)
            if c > NPQ:
                scores_out(2 * (c - NPQ) - 2)
                scores_out(2 * (c - NPQ) - 1)
        scores_out(2 * P_HEADS - 2)
        scores_out(2 * P_HEADS - 1)
        e.wait_ge(sc_out, 2 * P_HEADS)

        def top16(n, src, rest, vals, idx):
            for s in range(n):
                o.did(e.max(vals(s, 0), src(s)))
            o.wait()
            for s in range(n):
                o.did(e.max_index(idx(s, 0), vals(s, 0), src(s)))
                o.did(e.match_replace(rest(s), vals(s, 0), src(s), NEG))
            o.wait()
            for s in range(n):
                o.did(e.max(vals(s, 8), rest(s)))
            o.wait()
            for s in range(n):
                o.did(e.max_index(idx(s, 8), vals(s, 8), rest(s)))
            o.wait()

        H8 = P_HEADS
        for t in range(TT):
            top16(2 * H8, lambda s: sc[:, t, s, :], lambda s: cur[:, s, :],
                  lambda s, k: topv[:, s, k:k + 8], lambda s, k: topi[:, s, k:k + 8])
            o.did(e.tensor_copy(topf[:], topi[:]))
            tv = topv[:].rearrange("p (h i) k -> p h i k", i=2)
            tf = topf[:].rearrange("p (h i) k -> p h i k", i=2)
            grid = [P, H8, TOPK, TOPK]
            o.then(e.tensor_tensor(cand[:].rearrange("p h (a b) -> p h a b", a=TOPK),
                                   tv[:, :, 0, :].unsqueeze(3).broadcast_to(grid),
                                   tv[:, :, 1, :].unsqueeze(2).broadcast_to(grid), ALU.add))
            top16(H8, lambda s: cand[:, s, :], lambda s: cand2[:, s, :],
                  lambda s, k: best[:, s, k:k + 8], lambda s, k: bpos[:, s, k:k + 8])
            e.tensor_tensor(gate[:, 0], best[:], best[:, :, 0:1].broadcast_to([P, H8, TOPK]), ALU.subtract
                            ).then_inc(g_shift, 1)
            o.did(e.tensor_scalar(bab[:, 0], bpos[:], 4, None, ALU.logical_shift_right))
            o.then(e.tensor_scalar(bab[:, 1], bpos[:], TOPK - 1, None, ALU.bitwise_and))
            o.then(e.tensor_copy(babf[:], bab[:]))
            k16 = iota[:, 0:TOPK].unsqueeze(1).unsqueeze(1).broadcast_to(grid)
            picks = (cur, pick)
            if t >= 2:
                e.wait_ge(r_tr, t - 1)
            for i in range(2):
                eq = picks[i][:].rearrange("p s (r k) -> p (s r) k", k=TOPK).rearrange("p (h r) k -> p h r k", h=H8)
                o.then(e.tensor_tensor(eq, babf[:, i].unsqueeze(3).broadcast_to(grid), k16, ALU.is_equal))
                o.then(e.tensor_tensor(eq, eq, tf[:, :, i, :].unsqueeze(2).broadcast_to(grid), ALU.mult))
                e.tensor_reduce(R3[:, t % 2, i, :].rearrange("p (h r) -> p h r", h=H8), eq, AX_X, ALU.add).then_inc(r_done, 1)
            e.wait_ge(g_exp, t + 1)
            o.then(e.tensor_reduce(gsum[:, 0], gate[:, 1], AX_X, ALU.add))
            o.then(e.reciprocal(gsum[:, 1], gsum[:, 0]))
            e.tensor_tensor(R3[:, t % 2, 2, :].rearrange("p (h r) -> p h r", h=H8), gate[:, 1],
                            gsum[:, 1].unsqueeze(2).broadcast_to([P, H8, TOPK]), ALU.mult).then_inc(r_done, 1)
            e.wait_ge(r_done, 3 * (t + 1))
            e.wait_ge(r_tr, t + 1)
            e.tensor_copy(rt[:, :, t * P:(t + 1) * P], ps[:, 6, 0:3 * P].rearrange("p (r n) -> p r n", r=3)
                          ).then_inc(r_out, 1)

    def dve_onehots(e, b2):
        for q in range(2 * QPB):
            n = b2 * 2 * QPB + q
            wait_if(e, gq_mm, n - 1)
            for r in range(4):
                tok = n * 4 + r
                col = [rt[:, k, bass.ds(tok, 1)] for k in range(3)]
                e.tensor_scalar(oneI[:, q % 2, r, :], iota[:], col[0], col[2], ALU.is_equal, ALU.mult)
                ins = e.tensor_scalar(oneJ[:, q % 2, r, :], iota[:], col[1], None, ALU.is_equal)
            ins.then_inc(oh_done, 1)

    def pe_gates(e, b2):
        for q in range(2 * QPB):
            n = b2 * 2 * QPB + q
            e.wait_ge(oh_done, n + 1)
            wait_if(e, gq_out, n - 3)
            for r in range(4):
                ins = e.matmul(ps[:, q % 4, r * P:(r + 1) * P], oneJ[:, q % 2, r, :], oneI[:, q % 2, r, :],
                               start=True, stop=True)
            ins.then_inc(gq_mm, 1)

    def act_gates(e, b2):
        for q in range(2 * QPB):
            n = b2 * 2 * QPB + q
            s, qq = q // QPB, q % QPB
            if qq == 0:
                wait_if(e, gb_st[s], 16 * b2)
            e.wait_ge(gq_mm, n + 1)
            e.activation(Gst[:, s, :, 4 * qq:4 * qq + 4].rearrange("p i t -> p t i"),
                         ps[:, q % 4, :].rearrange("p (t i) -> p t i", t=4), ACT.Copy).then_inc(gq_out, 1)

    def sp_gates(e, b2):
        for s in range(2):
            e.wait_ge(gq_out, b2 * 2 * QPB + (s + 1) * QPB)
            e.dma_start(G_dram[bass.ds(b2 * 2 + s, 1)].rearrange("b j i t -> j (b i t)"),
                        Gst[:, s].rearrange("p i t -> p (i t)")).then_inc(gb_st[s], 16)

    def vw_slot(x):
        return x // GRP % 2 if x % GRP == 0 else x % GRP + 1

    def vw_free(e, E, x):
        if x % GRP == 0:
            wait_if(e, o_mm, 2 * E - 8)
        else:
            wait_if(e, o_mm, 2 * (E - x % GRP))

    def sp_experts(e, it):
        for x in range(8):
            E = it * 8 + x
            wait_if(e, t_mm, 2 * E - 6)
            e.dma_start(Uraw[:, x % 4, :], peer_u[bass.ds(E * P, P), :]).then_inc(u_in[x % 4], 16)

    def pool_experts(e, it):
        for x in range(8):
            E = it * 8 + x
            if x % GRP == 0:
                wait_if(e, w_mul, E - GRP)
                e.dma_start(Gt[:, x // GRP].rearrange("p b i t -> p b (i t)"),
                            G_dram[:, :, bass.ds(E, GRP), :].rearrange("b j i t -> j b (i t)")).then_inc(gt_in[x // GRP], 16)
            wait_if(e, vt_lo, E - 3)
            e.dma_start(Vraw[:, x % 4, :], peer_v[bass.ds(E * P, P), :]).then_inc(v_in[x % 4], 16)

    def landed(e, sems, E, x):
        n = len(sems)
        it, xx = (E - x % 8) * (16 // n), x % 8
        e.wait_ge(sems[xx % n], it + 16 * (xx // n + 1))

    def pe_turn_u(e, E, x):
        landed(e, u_in, E, x)
        wait_if(e, t_lo, 2 * E - 2)
        for hf in range(2):
            for k in range(4):
                ins = e.transpose(ps[:, 2 + 2 * (x % 2) + hf, k * P:(k + 1) * P],
                                  Uraw[:, x % 4, (4 * hf + k) * P:(4 * hf + k + 1) * P], ident[:])
            ins.then_inc(t_mm, 1)

    def pe_hidden(e, E, x):
        e.wait_ge(t_lo, 2 * E + 2)
        wait_if(e, h_gelu, E - 1)
        product3(e, ps[:, x % 2, :], [(UTh[:, x % 2, k, :], UTl[:, x % 2, k, :], actH[:, k, :], actL[:, k, :])
                                      for k in range(KD)]).then_inc(h_mm, 1)

    def pe_outputs(e, E, x):
        e.wait_ge(wt_lo, E)
        e.wait_ge(vt_lo, E)
        sl = [vw_slot((x - GRP + k) % 8) for k in range(GRP)]
        for b in range(2 * TT):
            t, hf = b // 2, b % 2
            wait_if(e, o_add, 2 * E - 8 + b - 1)
            ts, cs = slice(t * P, (t + 1) * P), slice(hf * 512, (hf + 1) * 512)
            product3(e, ps[:, 6 + b % 2, :], [(Wh[:, s, ts], Wl[:, s, ts], Vh[:, s, cs], Vl[:, s, cs]) for s in sl]
                     ).then_inc(o_mm, 1)

    def pe_step(e, E, x, last=False):
        pe_hidden(e, E, x)
        if not (last and x % 8 >= 6):
            pe_turn_u(e, E + 2, (x + 2) % 8)
        if x % GRP == 0 and not (isinstance(E, int) and E == 0):
            pe_outputs(e, E, x % 8)

    def act_turn_u(e, E, x):
        wait_if(e, h_mm, E - 1)
        for hf in range(2):
            e.wait_ge(t_mm, 2 * E + hf + 1)
            e.activation(UTh[:, x % 2, 4 * hf:4 * hf + 4, :], ps[:, 2 + 2 * (x % 2) + hf, :].rearrange("p (k n) -> p k n", k=4),
                         ACT.Copy).then_inc(t_hi, 1)

    def act_step(e, E, x, last=False):
        x8 = x % 8
        e.wait_ge(h_mm, E + 1)
        wait_if(e, w_mul, E - 1)
        e.activation(ga[:, x % 2, :], ps[:, x % 2, :], ACT.Gelu).then_inc(h_gelu, 1)
        if not (last and x8 >= 6):
            act_turn_u(e, E + 2, (x + 2) % 8)
        vw_free(e, E, x8)
        e.wait_ge(w_mul, E + 1)
        e.activation(Wh[:, vw_slot(x8), :], Wf[:, x % 2, :], ACT.Copy).then_inc(wt_hi, 1)
        landed(e, v_in, E, x)
        e.activation(Vh[:, vw_slot(x8), :], Vraw[:, x % 4, :], ACT.Copy).then_inc(vt_hi, 1)

    def dve_turn_u(e, E, x):
        for hf in range(2):
            e.wait_ge(t_hi, 2 * E + hf + 1)
            e.tensor_tensor(UTl[:, x % 2, 4 * hf:4 * hf + 4, :],
                            ps[:, 2 + 2 * (x % 2) + hf, :].rearrange("p (k n) -> p k n", k=4),
                            UTh[:, x % 2, 4 * hf:4 * hf + 4, :].bitcast(F32), ALU.subtract).then_inc(t_lo, 1)

    def dve_add_outputs(e, E):
        for b in range(2 * TT):
            t, hf = b // 2, b % 2
            e.wait_ge(o_mm, 2 * E - 8 + b + 1)
            dst = X[:, t, hf * 512:(hf + 1) * 512]
            e.tensor_tensor(dst, ps[:, 6 + b % 2, :], dst, ALU.add).then_inc(o_add, 1)

    def dve_step(e, E, x, last=False):
        x8 = x % 8
        if x8 % GRP == 0:
            landed(e, gt_in_by_tile, E, x)
        e.wait_ge(h_gelu, E + 1)
        wait_if(e, wt_lo, E - 1)
        e.tensor_tensor(Wf[:, x % 2, :].rearrange("p (b t) -> p b t", b=NTB), ga[:, x % 2, :].rearrange("p (b t) -> p b t", b=NTB),
                        Gt[:, x8 // GRP, :, x8 % GRP, :], ALU.mult).then_inc(w_mul, 1)
        if not (last and x8 >= 6):
            dve_turn_u(e, E + 2, (x + 2) % 8)
        e.wait_ge(wt_hi, E + 1)
        e.tensor_tensor(Wl[:, vw_slot(x8), :], Wf[:, x % 2, :], Wh[:, vw_slot(x8), :].bitcast(F32), ALU.subtract
                        ).then_inc(wt_lo, 1)
        e.wait_ge(vt_hi, E + 1)
        e.tensor_tensor(Vl[:, vw_slot(x8), :], Vraw[:, x % 4, :], Vh[:, vw_slot(x8), :].bitcast(F32), ALU.subtract
                        ).then_inc(vt_lo, 1)
        if x8 % GRP == 0 and not (isinstance(E, int) and E == 0):
            dve_add_outputs(e, E)

    class _ByTile:
        def __len__(self):
            return 8
        def __getitem__(self, x):
            return gt_in[x // GRP]
    gt_in_by_tile = _ByTile()

    def steps(e, step):
        step(e, 0, 0)
        step(e, 1, 1)
        for x in range(2, 10):
            step(e, x, x)
        with e.Fori(1, NITER - 1) as it:
            for x in range(2, 10):
                step(e, it * 8 + x, x)
        for x in range(2, 8):
            step(e, (NITER - 1) * 8 + x, x, last=True)


    with nc.Block() as block:
        @block.sync
        def _(e):
            sp_front(e)
            sp_gates(e, 0)
            with e.Fori(1, NTB // 2) as b2:
                sp_gates(e, b2)
            e.wait_ge(gb_st[0], 16 * NTB // 2)
            e.wait_ge(gb_st[1], 16 * NTB // 2)
            sp_experts(e, 0)
            with e.Fori(1, NITER) as it:
                sp_experts(e, it)
            for t in range(TT):
                e.wait_ge(f_out, t + 1)
                e.dma_start(out[0, t * P:(t + 1) * P, :], ost[:, t, :]).then_inc(f_st, 16)
            e.wait_ge(f_st, 16 * TT)

        @block.gpsimd
        def _(e):
            pool_front(e)
            e.wait_ge(v_done, NU)
            e.dma_start(skraw[:], peer_sub_keys.rearrange("i n d -> n i d")).then_inc(sk_in, 16)
            e.wait_ge(gb_st[0], 16 * NTB // 2)
            e.wait_ge(gb_st[1], 16 * NTB // 2)
            e.dma_start(wfin[:], norm_final_w.rearrange("(a n) -> a n", a=1).broadcast_to([P, D])).then_inc(wf_in, 16)
            pool_experts(e, 0)
            with e.Fori(1, NITER) as it:
                pool_experts(e, it)

        @block.tensor
        def _(e):
            pe_front(e)
            pe_ssd(e)
            e.wait_ge(ys_tok, 2 * NSC)
            for k in range(KD):
                pe_turn(e, "ys", k, lambda t: ztok[:, t, k * P:(k + 1) * P])
            e.wait_ge(ts_lo, TS["ys"] + KD)
            for c in range(first["pssd"], first["q"]):
                pe_channels(e, c, actH[:], actL[:])
            pe_attention(e)
            pe_merge(e)
            pe_routing(e)
            pe_gates(e, 0)
            with e.Fori(1, NTB // 2) as b2:
                pe_gates(e, b2)
            e.wait_ge(gq_out, S // 4)
            pe_turn_u(e, 0, 0)
            pe_turn_u(e, 1, 1)
            steps(e, pe_step)
            pe_outputs(e, E_TILES, 0)

        @block.scalar
        def _(e):
            o = Ordered(e, aco)
            act_front(e, o)
            act_ssd(e)
            act_pssd(e)
            act_attention(e)
            act_merge(e)
            act_routing(e)
            act_gates(e, 0)
            with e.Fori(1, NTB // 2) as b2:
                act_gates(e, b2)
            act_turn_u(e, 0, 0)
            act_turn_u(e, 1, 1)
            steps(e, act_step)
            for t in range(TT):
                e.wait_ge(o_add, 2 * E_TILES - 8 + 2 * (t + 1))
                e.activation(ost[:, t, :], X[:, t, :], ACT.Square, accum_out=stat[:, t:t + 1]).then_inc(f_sq, 1)
                e.wait_ge(f_sq, t + 1)
                e.activation(stat[:, 4 + t:5 + t], stat[:, t:t + 1], ACT.Sqrt, bias=epsc[:, 0:1], scale=1.0 / D
                             ).then_inc(f_rt, 1)

        @block.vector
        def _(e):
            o = Ordered(e, dvo)
            dve_front(e, o)
            dve_ssd(e, o)
            dve_pssd(e)
            dve_attention(e, o)
            dve_merge(e)
            dve_routing(e, o)
            e.wait_ge(r_out, TT)
            dve_onehots(e, 0)
            with e.Fori(1, NTB // 2) as b2:
                dve_onehots(e, b2)
            dve_turn_u(e, 0, 0)
            dve_turn_u(e, 1, 1)
            steps(e, dve_step)
            dve_add_outputs(e, E_TILES)
            e.wait_ge(wf_in, 16)
            for t in range(TT):
                e.wait_ge(f_rt, t + 1)
                o.then(e.reciprocal(stat[:, 8 + t:9 + t], stat[:, 4 + t:5 + t]))
                e.scalar_tensor_tensor(out=ost[:, t, :], in0=X[:, t, :], scalar=stat[:, 8 + t:9 + t], in1=wfin[:],
                                       op0=ALU.mult, op1=ALU.mult).then_inc(f_out, 1)


_INS = ["x", "positions", "norm_mix_w", "w_in", "conv_w", "conv_b", "dt_bias_fwd", "dt_bias_bwd", "a_log_fwd",
        "a_log_bwd", "d_skip", "ssd_norm_w", "q_a_norm_w", "w_q_b", "kv_a_norm_w", "w_kv_b", "w_proj_ssd",
        "w_proj_mla", "w_out", "norm_ffn_w", "peer_w_q", "peer_sub_keys", "peer_u", "peer_v", "norm_final_w"]


def kernel(**inputs):
    import concourse.bacc as bacc
    from concourse.bass_utils import run_bass_kernel_spmd

    nc = bacc.Bacc("TRN2", target_bir_lowering=False, num_devices=1)
    arrays = {f"in_{n}": np.ascontiguousarray(inputs[n]) for n in _INS}
    exps = np.arange(0, QK_ROPE, 2, dtype=np.float32) / np.float32(QK_ROPE)
    arrays["in_rope_inv"] = (np.float32(1.0) / np.float32(ROPE_THETA) ** exps).astype(np.float32)
    args = [nc.dram_tensor(k, a.shape, mybir.dt.from_np(a.dtype), kind="ExternalInput").ap() for k, a in arrays.items()]
    shape = arrays["in_x"].shape
    out = nc.dram_tensor("out_0", shape, F32, kind="ExternalOutput").ap()
    gates_dram = nc.dram_tensor("gates_dram", (2 * shape[2] // P, P, shape[1]), F32, kind="Internal").ap()
    G_dram = nc.dram_tensor("G_dram", (shape[1] // 32, P, P, 32), F32, kind="Internal").ap()
    block_kernel(nc, *args, out, gates_dram, G_dram)
    r = run_bass_kernel_spmd(nc, [arrays], core_ids=[0])
    return r.results[0]["out_0"]
```

```python
import math

import numpy as np

import concourse.bass as bass
from concourse import mybir

F32 = mybir.dt.float32
F32R = mybir.dt.float32r
BF16 = mybir.dt.bfloat16
U32 = mybir.dt.uint32
I32 = mybir.dt.int32
ALU = mybir.AluOpType
ACT = mybir.ActivationFunctionType
AX_X = mybir.AxisListType.X

P = 128
EPS = 1e-6
CHUNK = 128
N_GROUPS = 2
HEADDIM = 64
QK_NOPE, QK_ROPE, V_HEAD = 64, 32, 64
QK = QK_NOPE + QK_ROPE
ROPE_THETA = 10000.0
TOPK = 16
NEG = -3.0e38
MASKED = -1e30
ROUTE_WORK = 46.0
TWO_PI = 2.0 * math.pi
KB = 1024


class Ordered:

    def __init__(self, eng, sem):
        self.eng, self.sem, self.n, self.shift = eng, sem, 0, 0

    def did(self, ins):
        self.n += 1
        ins.then_inc(self.sem, 1)
        return self.n

    def wait(self, n=None):
        self.eng.wait_ge(self.sem, self.shift + (self.n if n is None else n))

    def then(self, ins):
        self.did(ins)
        self.wait()

    def again(self, turns, first, per):
        self.shift = (turns - first) * per

    def over(self, extra, per):
        self.n += (extra - 1) * per
        self.shift = 0


def wait_if(eng, sem, value):
    if not isinstance(value, int) or value > 0:
        eng.wait_ge(sem, value)


def block_kernel(nc, x, positions, norm_mix_w, w_in, conv_w, conv_b, dt_bias_fwd, dt_bias_bwd,
                 a_log_fwd, a_log_bwd, d_skip, ssd_norm_w, q_a_norm_w, w_q_b, kv_a_norm_w, w_kv_b,
                 w_proj_ssd, w_proj_mla, w_out, norm_ffn_w, peer_w_q, peer_sub_keys, peer_u, peer_v,
                 norm_final_w, rope_inv, out, gates_dram, G_dram, act_dram):
    _, S, D = x.shape
    TT = S // P
    KD = D // P
    D_INNER = ssd_norm_w.shape[0]
    HEADS = d_skip.shape[0]
    HPG = HEADS // N_GROUPS
    GD = D_INNER // N_GROUPS
    CONV_DIM = conv_b.shape[0]
    CT_N = CONV_DIM // P
    XS_CT = D_INNER // P
    Q_LORA, KV_LORA = q_a_norm_w.shape[0], kv_a_norm_w.shape[0]
    KQ, KKV = Q_LORA // P, KV_LORA // P
    A_HEADS = w_proj_mla.shape[0] // V_HEAD
    MID = 2 * HEADS + Q_LORA + KV_LORA + QK_ROPE
    Z0, XBC0 = 0, D_INNER
    MID0 = XBC0 + CONV_DIM
    GATE0 = MID0 + MID
    P_HEADS = peer_w_q.shape[1] // (2 * P)
    N_I = peer_u.shape[0] // P
    SCALE = float(QK) ** -0.5
    assert S == 512 and D == 1024 and P_HEADS * TOPK == P and N_I == P and CHUNK == P

    def at(name, kb, shape, dt=F32):
        return nc.alloc_sbuf_tensor_at(name, shape, dt, offset=int((17 + kb) * KB))

    ident = at("ident", 0, [P, P])
    ones = at("ones", 0.5, [P, P])
    triU = at("triU", 1, [P, P])
    triL = at("triL", 1.5, [P, P])
    iota = at("iota", 2, [P, P])
    identb = at("identb", 2.5, [P, P], BF16)
    maskF = at("maskF", 2.75, [P, P], BF16)
    maskB = at("maskB", 3, [P, P], BF16)
    vecs = at("vecs", 3.25, [P, P])
    vecT = at("vecT", 3.75, [P, P])
    dtb = at("dtb", 4.25, [P, 2 * HEADS])
    aneg = at("aneg", 4.375, [P, 2 * HEADS])
    dsk = at("dsk", 4.5, [P, HEADS])
    inv = at("inv", 4.625, [P, QK_ROPE // 2])
    posi = at("posi", 4.75, [P, TT], I32)
    posf = at("posf", 4.78125, [P, TT])
    stat = at("stat", 4.8125, [P, 64])
    trig = at("trig", 5.0625, [P, 6, TT, QK_ROPE // 2])
    sdt = at("sdt", 6.625, [P, 8, TT, 2 * HEADS])
    epsc = at("epsc", 10.75, [P, 4])
    rsum = at("rsum", 10.875, [P, 16])
    nmx = at("nmx", 10.9375, [P, 16])
    iotab = at("iotab", 11, [P, P], BF16)
    X = at("X", 12, [P, TT, D])
    actH = at("actH", 28, [P, KD, S], F32R)
    actL = at("actL", 44, [P, KD, S], F32R)
    wraw = at("wraw", 60, [P, 2, 2048])
    wH = at("wH", 76, [P, 2, 2048], F32R)
    wL = at("wL", 92, [P, 2, 2048], F32R)
    utok = at("utok", 108, [P, TT, D])
    ztok = at("ztok", 108, [P, TT, D_INNER])
    xtok = at("xtok", 124, [P, TT, D_INNER])
    BT = at("BT", 140, [P, N_GROUPS, S])
    CTt = at("CTt", 144, [P, N_GROUPS, S])
    Btok = at("Btok", 148, [P, TT, N_GROUPS * P])
    mid = at("mid", 152, [P, TT, MID])
    pre = at("pre", 163, [P, 2, S + 2])
    conv = at("conv", 167.5, [P, 2, S])
    cact = at("cact", 171.5, [P, 2, S])
    gst = at("gst", 176, [P, 2, S])
    qaH = at("qaH", 180, [P, KQ, S], F32R)
    qaL = at("qaL", 186, [P, KQ, S], F32R)
    kaH = at("kaH", 192, [P, KKV, S], F32R)
    kaL = at("kaL", 196, [P, KKV, S], F32R)
    kropeT = at("kropeT", 200, [P, S])
    krot = at("krot", 202, [P, TT, QK])
    xd = at("xd", 60, [P, 2, D_INNER])
    LM = at("LM", 76, [P, 2, 2, 4, P])
    xdec = at("xdec", 92, [P, 2, D_INNER])
    ya = at("ya", 92, [P, 4, GD])
    prev = at("prev", 152, [P, 2, N_GROUPS, 3, GD])
    CB = at("CB", 202, [P, S // CHUNK, N_GROUPS, P])
    mS = at("mS", 108, [P, KD, S])
    mH = at("mH", 140, [P, KD, S], F32R)
    mL = at("mL", 156, [P, KD, S], F32R)
    mtmp = at("mtmp", 172, [P, 2, S])
    gld = at("gld", 176, [P, 2, S])
    ytok = at("ytok", 124, [P, TT, A_HEADS * V_HEAD])
    qrot = at("qrot", 140, [P, TT, 2, QK])
    rtmp = at("rtmp", 143, [P, 4, TT, 2, QK_ROPE // 2])
    QT = at("QT", 145, [P, 2, 2, S])
    KT = at("KT", 153, [P, 2, 2, S])
    Vt = at("Vt", 161, [P, 2, TT, 2, V_HEAD])
    Pr = at("Pr", 165, [P, 2, S])
    PT = at("PT", 169, [P, 2, TT, P])

    u2tok = at("u2tok", 108, [P, TT, D])
    rt = at("rt", 108, [P, 3, S])
    sc = at("sc", 124, [P, TT, 2 * P_HEADS, P])
    cur = at("cur", 156, [P, 2 * P_HEADS, P])
    pick = at("pick", 164, [P, 2 * P_HEADS, P])
    qT = at("qT", 172, [P, 2, S])
    cand = at("cand", 176, [P, P_HEADS, TOPK * TOPK])
    cand2 = at("cand2", 184, [P, P_HEADS, TOPK * TOPK])
    skraw = at("skraw", 192, [P, 2, P])
    skT = at("skT", 193, [P, 2, P])
    topv = at("topv", 194, [P, 2 * P_HEADS, TOPK])
    topi = at("topi", 195, [P, 2 * P_HEADS, TOPK], U32)
    topf = at("topf", 196, [P, 2 * P_HEADS, TOPK])
    best = at("best", 197, [P, P_HEADS, TOPK])
    bpos = at("bpos", 197.5, [P, P_HEADS, TOPK], U32)
    bab = at("bab", 198, [P, 2, P_HEADS, TOPK], U32)
    babf = at("babf", 199, [P, 2, P_HEADS, TOPK])
    gate = at("gate", 200, [P, 2, P_HEADS, TOPK])
    gsum = at("gsum", 201, [P, 2, P_HEADS])
    R3 = at("R3", 201.25, [P, 3, P_HEADS * TOPK])
    scur = at("scur", 114, [P, 2 * P_HEADS, P])
    gb16 = at("gb16", 199, [P, S], BF16)
    oneE = at("oneE", 166, [P, 2, 4, P], BF16)
    ib16 = at("ib16", 197, [P, S], BF16)
    jb16 = at("jb16", 198, [P, S], BF16)
    rest1 = at("rest1", 122, [P, S])
    rest2 = at("rest2", 202.75, [P, S])
    TB = 32
    NTB = S // TB
    Gst = at("Gst", 124, [P, 2, N_I, TB])
    oneI = at("oneI", 156, [P, 2, 3, 4, P], BF16)
    oneJ = at("oneJ", 164, [P, 2, 4, P], BF16)
    GRP = 4
    Uraw = at("Uraw", 60, [P, 4, D])
    UTh = at("UTh", 76, [P, 2, KD, P], F32R)
    UTl = at("UTl", 84, [P, 2, KD, P], F32R)
    ga = at("ga", 92, [P, 4, S])
    Vh = [at("Vh0", 100, [P, GRP, D], F32R), at("Vh1", 28, [P, GRP, D], F32R)]
    Vl = [at("Vl0", 116, [P, GRP, D], F32R), at("Vl1", 44, [P, GRP, D], F32R)]
    Wh = [at("Wh0", 132, [P, GRP, S], F32R), at("Wh1", 60, [P, GRP, S], F32R)]
    Wl = [at("Wl0", 140, [P, GRP, S], F32R), at("Wl1", 68, [P, GRP, S], F32R)]
    Vraw = at("Vraw", 148, [P, 4, D])
    hid = at("hid", 164, [P, 4, S])
    Gt = at("Gt", 172, [P, 2, NTB, GRP, TB])
    Wf = at("Wf", 188, [P, 2, S])
    wfin = at("wfin", 192, [P, D])
    ost = at("ost", 76, [P, TT, D])

    def sem(name):
        return nc.alloc_semaphore(name)

    ps = nc.alloc_psum_tensor("ps", [P, 8, 512], F32)

    def cols(w, lo, n):
        return w.rearrange("(k p) n -> p k n", p=P)[:, :, lo:lo + n]

    kvv = w_kv_b.rearrange("(k p) n -> p k n", p=P)
    chunks = []
    for j in range(CONV_DIM // 256):
        chunks.append(("conv", j, cols(w_in, XBC0 + 256 * j, 256), KD, 256, "act"))
    for j in range((MID + 255) // 256):
        chunks.append(("mid", j, cols(w_in, MID0 + 256 * j, min(256, MID - 256 * j)), KD, min(256, MID - 256 * j), "dve"))
    for j in range(D_INNER // 256):
        chunks.append(("z", j, cols(w_in, Z0 + 256 * j, 256), KD, 256, "act"))
    for j in range(2 * KD):
        chunks.append(("gate", j, cols(w_in, GATE0 + P * j, P), KD, P, "act"))
    for u in range(A_HEADS // 2):
        chunks.append(("q", u, cols(w_q_b, 2 * QK * u, 2 * QK), KQ, 2 * QK, "act"))
        chunks.append(("kv", u, kvv[:, :, 256 * u:256 * u + 256], KKV, 256, "dve"))
    for j in range(D // 256):
        chunks.append(("pssd", j, cols(w_proj_ssd, 256 * j, 256), KD, 256, "dve"))
    for j in range(D // 256):
        chunks.append(("pmla", j, cols(w_proj_mla, 256 * j, 256), KD, 256, "dve"))
    for j in range(D // 256):
        chunks.append(("out", j, cols(w_out, 256 * j, 256), KD, 256, "dve"))
    for j in range(P_HEADS * 2 * P // 256):
        chunks.append(("pq", j, cols(peer_w_q, 256 * j, 256), KD, 256, "act"))
    NCH = len(chunks)
    QA_BANK, KV_BANK = 2, 0
    NARROW = ("gate", "q", "kv")
    first = {}
    for c, ch in enumerate(chunks):
        first.setdefault(ch[0], c)
    assert first["gate"] % 2 == 1 and first["q"] % 2 == 1
    outs = {"act": 0, "dve": 0}
    taken = []
    for ch in chunks:
        outs[ch[5]] += 2
        taken.append((ch[5], outs[ch[5]]))

    def part(t, c):
        stage, _, _, kt, w, _ = chunks[c]
        return t[:, 1, c % 2 * 1024:c % 2 * 1024 + kt * w] if stage in NARROW else t[:, c % 2, 0:kt * w]

    def raw(c):
        return part(wraw, c)

    def part3(t, c):
        return part(t, c).rearrange("p (k n) -> p k n", k=chunks[c][3])

    small_in = sem("small_in")
    x_in = [sem(f"x_in{t}") for t in range(TT)]
    w_inq = [sem(f"w_in{s}") for s in range(2)]
    w_hi = sem("w_hi")
    w_lo = sem("w_lo")
    gemm_done = sem("gemm_done")
    v_done = sem("v_done")
    out_act = sem("out_act")
    out_dve = sem("out_dve")
    const_ready = sem("const_ready")
    vt_tr = sem("vt_tr")
    vt_ready = sem("vt_ready")
    x_sq = sem("x_sq")
    x_rt = sem("x_rt")
    u_tok = sem("u_tok")
    ts_tr = sem("ts_tr")
    ts_hi = sem("ts_hi")
    ts_lo = sem("ts_lo")
    pre_ready = sem("pre_ready")
    conv_done = sem("conv_done")
    cact_done = sem("cact_done")
    ct_tr = sem("ct_tr")
    ct_out = sem("ct_out")
    mid_done = sem("mid_done")
    mid_act = sem("mid_act")
    acs_mm = sem("acs_mm")
    a_ready = sem("a_ready")
    dvo = sem("dve_order")
    aco = sem("act_order")
    poo = sem("pool_order")
    qk_tok = sem("qk_tok")
    kr_tr = sem("kr_tr")
    kr_out = sem("kr_out")
    g_store = sem("g_store")
    g_sig = sem("g_sig")
    g_load = [sem(f"g_load{s}") for s in range(2)]

    usedq = {}

    def chunk_used(e, c):
        if c < 0:
            return
        if chunks[c][0] == "kv":
            e.wait_ge(v_done, chunks[c][1] + 1)
        else:
            e.wait_ge(gemm_done, 2 * (c + 1))

    V_MIX, V_CW, V_CB = 0, KD, KD + 3 * CT_N
    V_SSD = V_CB + CT_N
    V_QA = V_SSD + KD
    V_KA = V_QA + KQ
    V_FFN = V_KA + KKV
    NV = V_FFN + KD
    TS = {}
    n = 0
    for name, kt in (("u", KD), ("qa", KQ), ("ka", KKV), ("ys", KD), ("ym", KD), ("u2", KD)):
        TS[name] = n
        n += kt

    def ts_bank(n):
        return 4 + n % 2

    def pe_turn(e, name, k, src):
        n = TS[name] + k
        wait_if(e, ts_lo, n - 1)
        for t in range(TT):
            ins = e.transpose(ps[:, ts_bank(n), t * P:(t + 1) * P], src(t), ident[:])
        ins.then_inc(ts_tr, 1)

    def act_turn(e, name, k, hi, col):
        n = TS[name] + k
        e.wait_ge(ts_tr, n + 1)
        scale = 1.0 if col is None else vecT[:, col + k:col + k + 1]
        e.activation(hi, ps[:, ts_bank(n), :], ACT.Copy, scale=scale).then_inc(ts_hi, 1)

    def dve_turn(e, name, k, hi, lo, col):
        n = TS[name] + k
        e.wait_ge(ts_hi, n + 1)
        scale = 1.0 if col is None else vecT[:, col + k:col + k + 1]
        e.scalar_tensor_tensor(out=lo, in0=ps[:, ts_bank(n), :], scalar=scale, in1=hi.bitcast(F32),
                               op0=ALU.mult, op1=ALU.subtract).then_inc(ts_lo, 1)

    def act_hi(e, c):
        if c >= NCH:
            return
        e.wait_ge(w_inq[c % 2], 16 * (c // 2 + 1))
        chunk_used(e, c - 1 if c == first["pssd"] else c - 2)
        e.activation(part(wH, c), raw(c), ACT.Copy).then_inc(w_hi, 1)

    def dve_lo(e, c):
        if c >= NCH:
            return
        e.wait_ge(w_hi, c + 1)
        e.tensor_tensor(part(wL, c), raw(c), part(wH, c).bitcast(F32), ALU.subtract).then_inc(w_lo, 1)

    def pe_weights(e, c):
        e.wait_ge(w_lo, c + 1)
        if c >= 2:
            who, n = taken[c - 1 if c == first["q"] else c - 2]
            e.wait_ge(out_act if who == "act" else out_dve, n)

    def product3(e, out_ap, pairs, first_mm=True, last_mm=True):
        n = 3 * len(pairs)
        i = 0
        for lh, ll, rh, rl in pairs:
            for a, b in ((lh, rh), (lh, rl), (ll, rh)):
                ins = e.matmul(out_ap, a, b, start=first_mm and i == 0, stop=last_mm and i == n - 1)
                i += 1
        return ins

    def pe_channels(e, c, hi, lo):
        pe_weights(e, c)
        wh, wl = part3(wH, c), part3(wL, c)
        for m in range(2):
            cs = slice(m * P, (m + 1) * P)
            product3(e, ps[:, 2 * (c % 2) + m, :],
                     [(wh[:, k, cs], wl[:, k, cs], hi[:, k, :], lo[:, k, :]) for k in range(chunks[c][3])]
                     ).then_inc(gemm_done, 1)

    def pe_turn_channels(e, name, c, src):
        pe_turn(e, name, 0, src(0))
        pe_turn(e, name, 1, src(1))
        pe_weights(e, c)
        wh, wl = part3(wH, c), part3(wL, c)
        for k in range(KD):
            e.wait_ge(ts_lo, TS[name] + k + 1)
            for m in range(2):
                cs = slice(m * P, (m + 1) * P)
                ins = product3(e, bank(c, m), [(wh[:, k, cs], wl[:, k, cs], actH[:, k, :], actL[:, k, :])],
                               k == 0, k == KD - 1)
                if k == KD - 1:
                    ins.then_inc(gemm_done, 1)
            if k + 2 < KD:
                pe_turn(e, name, k + 2, src(k + 2))

    def pe_tokens(e, c, hi, lo):
        pe_weights(e, c)
        wh, wl = part3(wH, c), part3(wL, c)
        w = chunks[c][4]
        for m in range(2):
            for h in range(2):
                ts = slice((2 * m + h) * P, (2 * m + h + 1) * P)
                ins = product3(e, ps[:, 2 * (c % 2) + m, h * w:(h + 1) * w],
                               [(hi[:, k, ts], lo[:, k, ts], wh[:, k, :], wl[:, k, :])
                                for k in range(chunks[c][3])])
            ins.then_inc(gemm_done, 1)

    def pe_gate(e, c):
        e.wait_ge(w_lo, c + 1)
        e.wait_ge(out_act, taken[c - 2 if c > first["gate"] + 1 else first["gate"] - 1][1])
        wh, wl = part3(wH, c), part3(wL, c)
        product3(e, gate_bank(c), [(wh[:, k, :], wl[:, k, :], actH[:, k, :], actL[:, k, :]) for k in range(KD)]
                 ).then_inc(gemm_done, 2)

    def gate_bank(c):
        return ps[:, 2 + c % 2, :]

    def bank(c, m):
        return ps[:, 2 * (c % 2) + m, :]

    def bank_tokens(c, m):
        w = chunks[c][4]
        return ps[:, 2 * (c % 2) + m, 0:2 * w].rearrange("p (t n) -> p t n", t=2)


    acs_out = sem("acs_out")
    acs_exp = sem("acs_exp")
    dd_ready = sem("dd_ready")
    xdec_ready = sem("xdec_ready")
    st_mm = sem("st_mm")
    st_out = sem("st_out")
    xd_ready = sem("xd_ready")
    cb_mm = sem("cb_mm")
    cb_out = sem("cb_out")
    lr_mm = sem("lr_mm")
    lx_exp = sem("lx_exp")
    m_done = sem("m_done")
    yd_mm = sem("yd_mm")
    yo_mm = sem("yo_mm")
    ysum = sem("ysum")
    ysq = sem("ysq")
    ys_rt = sem("ys_rt")
    ys_tok = sem("ys_tok")
    g_st = [sem(f"g_st{s}") for s in range(2)]
    qrot_done = sem("qrot_done")
    kt_out = sem("kt_out")
    v_out = sem("v_out")
    q_tr = sem("q_tr")
    q_out = sem("q_out")
    s_mm = sem("s_mm")
    mx_done = sem("mx_done")
    e_done = sem("e_done")
    p_tr = sem("p_tr")
    p_out = sem("p_out")
    pv_mm = sem("pv_mm")
    y_done = sem("y_done")
    m_sum = sem("m_sum")
    m_hi = sem("m_hi")
    m_lo = sem("m_lo")

    NSC = S // CHUNK
    HD = HEADDIM

    def heads(ap):
        return ap.rearrange("p (h n) -> p h n", n=HD)

    def over(ap, n):
        return ap.unsqueeze(2).broadcast_to([ap.shape[0], ap.shape[1], n])

    def turned_bank(h):
        return (QA_BANK + 1, KV_BANK)[h]

    attn = [(u, h, t) for u in range(A_HEADS // 2) for h in range(2) for t in range(TT)]
    NU = A_HEADS // 2

    def sp_front(e):
        for t in range(TT):
            e.dma_start(X[:, t, :], x[0, t * P:(t + 1) * P, :]).then_inc(x_in[t], 16)
        for c in range(2):
            e.dma_start(raw(c).rearrange("p (k n) -> p k n", k=chunks[c][3]), chunks[c][2]).then_inc(w_inq[c], 16)
        rows = [(norm_mix_w, V_MIX), (conv_w.rearrange("r c -> (r c)"), V_CW), (conv_b, V_CB), (ssd_norm_w, V_SSD),
                (q_a_norm_w, V_QA), (kv_a_norm_w, V_KA), (norm_ffn_w, V_FFN)]
        for v, r in rows:
            n = v.shape[0] // P
            e.dma_start(vecs[r:r + n, :], v.rearrange("(r n) -> r n", n=P)).then_inc(small_in, 16)
        for v, dst in ((dt_bias_fwd, dtb[:, 0:HEADS]), (dt_bias_bwd, dtb[:, HEADS:2 * HEADS]),
                       (a_log_fwd, aneg[:, 0:HEADS]), (a_log_bwd, aneg[:, HEADS:2 * HEADS]),
                       (d_skip, dsk[:]), (rope_inv, inv[:])):
            e.dma_start(dst, v.rearrange("(a n) -> a n", a=1).broadcast_to([P, v.shape[0]])).then_inc(small_in, 16)
        e.dma_start(posi[:], positions.rearrange("a (t p) -> p (a t)", p=P), allow_slow_non_contiguous=True).then_inc(small_in, 16)
        for c in range(2, NCH):
            e.wait_ge(w_lo, c if c == first["pssd"] else c - 1)
            e.dma_start(raw(c).rearrange("p (k n) -> p k n", k=chunks[c][3]), chunks[c][2]).then_inc(w_inq[c % 2], 16)

    SMALL = 16 * 14

    def pool_front(e):
        o = Ordered(e, poo)
        e.memset(ident[:], 0.0).then_inc(poo, 1)
        e.memset(triU[:], 0.0).then_inc(poo, 1)
        e.memset(triL[:], 0.0).then_inc(poo, 1)
        e.memset(ones[:], 1.0).then_inc(poo, 1)
        e.memset(maskF[:], 0.0).then_inc(poo, 1)
        e.memset(maskB[:], 0.0).then_inc(poo, 1)
        o.n = 6
        o.did(e.memset(epsc[:, 0:1], EPS))
        o.did(e.memset(epsc[:, 1:2], math.pi / 2))
        o.did(e.memset(pre[:], 0.0))
        o.did(e.memset(krot[:], 0.0))
        o.did(e.iota(iota[:], [[1, P]], base=0, channel_multiplier=0, allow_small_or_imprecise_dtypes=True))
        o.wait()
        def sel(t, op, fill, sign=1):
            return e.affine_select(out=t[:], in_=t[:], compare_op=op, fill=fill, base=0, pattern=[[-sign, P]],
                                   channel_multiplier=sign)
        o.did(sel(ident, ALU.not_equal, 1.0))
        o.did(sel(triU, ALU.is_gt, 1.0))
        o.did(sel(triL, ALU.is_gt, 1.0, -1))
        o.did(sel(maskF, ALU.is_ge, MASKED, -1))
        o.did(sel(maskB, ALU.is_ge, MASKED, 1))
        o.wait()
        e.tensor_copy(identb[:], ident[:]).then_inc(const_ready, 1)
        e.wait_ge(const_ready, 1)
        for i in range(2 * KD):
            e.wait_ge(out_act, taken[first["gate"] + i][1])
            e.dma_start(gates_dram[i], gst[:, i % 2, :]).then_inc(g_st[i % 2], 16)
        for i in range(2 * KD):
            if i == 0:
                e.wait_ge(g_st[0], 16 * KD)
                e.wait_ge(g_st[1], 16 * KD)
                e.wait_ge(ysq, 2 * NSC)
            if i >= 2:
                c = first["pssd"] + (i - 2) // 2 if i - 2 < KD else first["pmla"] + (i - 2 - KD) // 2
                e.wait_ge(out_dve, taken[c][1] - 1 + i % 2)
            e.dma_start(gld[:, i % 2, :], gates_dram[i]).then_inc(g_load[i % 2], 16)

    def pe_front(e):
        e.wait_ge(const_ready, 1)
        e.wait_ge(small_in, SMALL)
        e.transpose(ps[:, 6, 0:NV], vecs[0:NV, :], ident[0:NV, 0:NV]).then_inc(vt_tr, 1)
        e.wait_ge(u_tok, TT)
        pe_turn_channels(e, "u", 0, lambda k: lambda t: utok[:, t, k * P:(k + 1) * P])

        def turn_conv(ct):
            e.wait_ge(cact_done, ct + 1)
            wait_if(e, ct_out, ct - 1)
            src = cact[:, ct % 2, :] if ct < XS_CT else BT[:, ct - XS_CT, :]
            for t in range(TT):
                ins = e.transpose(ps[:, 4 + ct % 2, t * P:(t + 1) * P], src[:, t * P:(t + 1) * P], ident[:])
            ins.then_inc(ct_tr, 1)

        for c, (stage, j, *_) in enumerate(chunks[:first["gate"]]):
            if stage == "conv":
                if c >= 1:
                    pe_channels(e, c, actH[:], actL[:])
            else:
                pe_tokens(e, c, actH[:], actL[:])
            if stage == "conv" and j >= 1:
                turn_conv(2 * j - 2)
                turn_conv(2 * j - 1)
            if stage == "z" and j == 2:
                e.wait_ge(a_ready, 1)
                a = sdt[:, 1]
                e.matmul(ps[:, 6, 0:64], triU[:], a[:, :, 0:HEADS], start=True, stop=True)
                e.matmul(ps[:, 6, 64:128], triL[:], a[:, :, HEADS:2 * HEADS], start=True, stop=True)
                e.matmul(ps[:, 6, 128:256], ones[:], a[:], start=True, stop=True).then_inc(acs_mm, 1)
            if stage == "z" and j == 1:
                e.wait_ge(ct_out, XS_CT + N_GROUPS)
                e.wait_ge(qk_tok, 2 * TT + 2)
                for t in range(TT):
                    ins = e.transpose(ps[0:QK, 7, t * P:(t + 1) * P], krot[:, t, :], ident[:])
                ins.then_inc(kr_tr, 1)
                for k in range(KQ):
                    pe_turn(e, "qa", k, lambda t: mid[:, t, 2 * HEADS + k * P:2 * HEADS + (k + 1) * P])
                for k in range(KKV):
                    pe_turn(e, "ka", k, lambda t: mid[:, t, 2 * HEADS + Q_LORA + k * P:2 * HEADS + Q_LORA + (k + 1) * P])

    scan = [("state", i) for i in range(NSC - 1)] + [("y", n) for n in range(4 * NSC)]
    beside = {s: first["gate"] + i for i, s in enumerate(s for s in range(len(scan)) if s < 2 * KD)}
    assert len(beside) == 2 * KD

    def pe_ssd(e):
        def states(i):
            e.wait_ge(xdec_ready, 2 * (i + 1))
            for d in range(2):
                c = i if d == 0 else NSC - 1 - i
                for g in range(N_GROUPS):
                    n = 4 * i + 2 * d + g
                    wait_if(e, st_out, n - 1)
                    if n < 2:
                        e.wait_ge(kr_out, 1)
                        e.wait_ge(acs_exp, 3)
                    e.matmul(ps[:, 6 + n % 2, :], Btok[:, c, g * P:(g + 1) * P], xdec[:, d, g * GD:(g + 1) * GD],
                             start=True, stop=True).then_inc(st_mm, 1)

        def rows(n):
            c, g, hf = n // 4, n // 2 % 2, n % 2
            wait_if(e, lx_exp, n)
            for d in range(2):
                b = ps[:, d, :]
                mask = (maskF, maskB)[d][:].unsqueeze(1).broadcast_to([P, 4, P])
                e.matmul(b.rearrange("p (h n) -> p h n", h=4), identb[:], mask, start=True, stop=False)
                for h in range(4):
                    col = d * HEADS + g * HPG + hf * 4 + h
                    ins = e.matmul(b[:, h * P:(h + 1) * P], sdt[:, 1, c, col:col + 1].broadcast_to([P, P]),
                                   (triU, triL)[d][:], start=False, stop=h == 3)
            ins.then_inc(lr_mm, 1)

        def outputs(n):
            c, g, hf = n // 4, n // 2 % 2, n % 2
            tok = slice(c * P, (c + 1) * P)
            e.wait_ge(m_done, n + 1)
            e.wait_ge(xd_ready, 2 * (c + 1))
            e.wait_ge(cb_out, 1)
            if hf == 0:
                wait_if(e, ysum, 2 * c + g - 1)
            for h in range(4):
                hh = g * HPG + hf * 4 + h
                o = ps[:, 4 + g, (hf * 4 + h) * HD:(hf * 4 + h + 1) * HD]
                for d in range(2):
                    ins = e.matmul(o, LM[:, n % 2, d, h, :], xd[:, d, hh * HD:(hh + 1) * HD], start=d == 0, stop=d == 1)
            ins.then_inc(yd_mm, 1)
            if hf == 1:
                wait_if(e, ysum, 2 * c + g)
                e.wait_ge(st_out, 4 * (NSC - 1))
                if c > 0:
                    ins = e.matmul(ps[:, 7, :], CTt[:, g, tok], prev[:, 0, g, c - 1, :], start=True, stop=True)
                if c < NSC - 1:
                    ins = e.matmul(ps[:, 6, :], CTt[:, g, tok], prev[:, 1, g, NSC - 2 - c, :], start=True, stop=True)
                ins.then_inc(yo_mm, 1)

        for s, (kind, n) in enumerate(scan):
            if s in beside:
                pe_gate(e, beside[s])
            if s == 0:
                e.wait_ge(ts_lo, TS["ka"] + KKV)
                for c in range(NSC):
                    for g in range(N_GROUPS):
                        tok, at = slice(c * P, (c + 1) * P), (c % 2 * N_GROUPS + g) * P
                        ins = e.matmul(ps[:, 4 + c // 2, at:at + P], BT[:, g, tok], CTt[:, g, tok], start=True, stop=True)
                ins.then_inc(cb_mm, 1)
            if kind == "state":
                states(n)
            if s + 1 < len(scan) and scan[s + 1][0] == "y":
                rows(scan[s + 1][1])
            if kind == "y":
                outputs(n)

    def pe_attention(e):
        def queries_keys(u):
            c = first["q"] + 2 * u
            if u >= 1:
                e.wait_ge(v_out, u)
                e.wait_ge(q_out, 2 * u)
            pe_tokens(e, c, qaH[:], qaL[:])
            c += 1
            pe_weights(e, c)
            wh, wl = part3(wH, c), part3(wL, c)
            for h in range(2):
                cs = slice(h * P, (h + 1) * P)
                product3(e, bank(c, h), [(wh[:, k, cs], wl[:, k, cs], kaH[:, k, :], kaL[:, k, :]) for k in range(KKV)]
                         ).then_inc(gemm_done, 1)

        def values_turn(u):
            c = first["q"] + 2 * u + 1
            wh, wl = part3(wH, c), part3(wL, c)
            e.wait_ge(out_act, taken[c - 1][1])
            wh, wl = (w.rearrange("p k (h n) -> p k h n", h=2)[:, :, :, QK_NOPE:] for w in (wh, wl))
            for t in range(TT):
                ins = product3(e, ps[:, QA_BANK, 2 * t * V_HEAD:2 * (t + 1) * V_HEAD].rearrange("p (h n) -> p h n", h=2),
                               [(kaH[:, k, t * P:(t + 1) * P], kaL[:, k, t * P:(t + 1) * P], wh[:, k], wl[:, k])
                                for k in range(KKV)])
            ins.then_inc(v_done, 1)
            e.wait_ge(qrot_done, 2 * (u + 1))
            for h in range(2):
                if h == 1:
                    e.wait_ge(out_dve, taken[c][1])
                for t in range(TT):
                    ins = e.transpose(ps[0:QK, turned_bank(h), t * P:(t + 1) * P], qrot[:, t, h, :], ident[:])
                ins.then_inc(q_tr, 1)

        def score(n):
            u, h, t = attn[n]
            wait_if(e, e_done, n - 1)
            if h == 0 and t == 0:
                e.wait_ge(q_out, 2 * (u + 1))
                e.wait_ge(out_dve, taken[first["q"] + 2 * u + 1][1])
            e.matmul(ps[:, 4 + n % 2, :], QT[0:QK, u % 2, h, t * P:(t + 1) * P], KT[0:QK, u % 2, h, :],
                     start=True, stop=True).then_inc(s_mm, 1)

        def weigh(n):
            u, h, t = attn[n]
            e.wait_ge(p_out, n + 1)
            if h == 0 and t == 0:
                e.wait_ge(v_out, u + 1)
            if t == 0:
                wait_if(e, y_done, n // TT)
            for k in range(TT):
                ins = e.matmul(ps[:, 7, t * V_HEAD:(t + 1) * V_HEAD], PT[:, n % 2, k, :],
                               Vt[:, u % 2, k, h, :], start=k == 0, stop=k == TT - 1)
            ins.then_inc(pv_mm, 1)

        queries_keys(0)
        values_turn(0)
        e.wait_ge(ysum, 2 * NSC)
        score(0)
        for n, (u, h, t) in enumerate(attn):
            if t == 0 and u + 1 < NU:
                (queries_keys if h == 0 else values_turn)(u + 1)
            if n + 1 < len(attn):
                score(n + 1)
            e.wait_ge(e_done, n + 1)
            wait_if(e, p_out, n)
            for k in range(TT):
                ins = e.transpose(ps[:, 6, k * P:(k + 1) * P], Pr[:, n % 2, k * P:(k + 1) * P], ident[:])
            ins.then_inc(p_tr, 1)
            if n >= 1:
                weigh(n - 1)
        weigh(len(attn) - 1)

    def pe_merge(e):
        e.wait_ge(ys_tok, 2 * NSC)
        pe_turn_channels(e, "ys", first["pssd"], lambda k: lambda t: ztok[:, t, k * P:(k + 1) * P])
        for c in range(first["pssd"] + 1, first["pmla"]):
            pe_channels(e, c, actH[:], actL[:])
        e.wait_ge(y_done, A_HEADS)
        pe_turn_channels(e, "ym", first["pmla"], lambda k: lambda t: ytok[:, t, k * P:(k + 1) * P])
        for c in range(first["pmla"] + 1, first["out"]):
            pe_channels(e, c, actH[:], actL[:])
        e.wait_ge(m_lo, KD)
        for c in range(first["out"], first["pq"]):
            pe_tokens(e, c, mH[:], mL[:])

    def act_front(e, o):
        for t in range(TT):
            e.wait_ge(x_in[t], 16)
            e.activation(utok[:, t, :], X[:, t, :], ACT.Square, accum_out=stat[:, t:t + 1]).then_inc(x_sq, 1)
        e.wait_ge(x_sq, TT)
        e.wait_ge(const_ready, 1)
        e.activation(stat[:, 4:8], stat[:, 0:4], ACT.Sqrt, bias=epsc[:, 0:1], scale=1.0 / D).then_inc(x_rt, 1)
        e.wait_ge(small_in, SMALL)
        e.activation(sdt[:, 6, 0, :], aneg[:], ACT.Exp).then_inc(mid_act, 1)
        act_hi(e, 0)
        act_hi(e, 1)
        e.wait_ge(vt_ready, 1)
        for k in range(KD):
            act_turn(e, "u", k, actH[:, k, :], V_MIX)

        def silu_conv(ct):
            e.wait_ge(conv_done, ct + 1)
            wait_if(e, ct_tr, ct - 1 if ct < XS_CT else 0)
            dst = cact[:, ct % 2, :] if ct < XS_CT else BT[:, ct - XS_CT, :] if ct < XS_CT + N_GROUPS \
                else CTt[:, ct - XS_CT - N_GROUPS, :]
            e.activation(dst, conv[:, ct % 2, :], ACT.Silu).then_inc(cact_done, 1)

        for c, (stage, j, *_) in enumerate(chunks[:first["gate"]]):
            if c > 0:
                act_hi(e, c + 1)
            if stage == "conv":
                for m in range(2):
                    ct = 2 * j + m
                    e.wait_ge(gemm_done, 2 * c + m + 1)
                    wait_if(e, conv_done, ct - 1)
                    e.activation(pre[:, m, 1:S + 1], bank(c, m), ACT.Copy).then_inc(out_act, 1)
                    if ct >= 1:
                        silu_conv(ct - 1)
            if stage == "mid" and j == 0:
                silu_conv(CT_N - 1)
            if stage == "z":
                for m in range(2):
                    e.wait_ge(gemm_done, 2 * c + m + 1)
                    e.activation(ztok[:, 2 * m:2 * m + 2, j * 256:(j + 1) * 256], bank_tokens(c, m), ACT.Silu
                                 ).then_inc(out_act, 1)
            if stage == "z" and j == 0:
                e.wait_ge(mid_done, 1)
                e.activation(sdt[:, 7], sdt[:, 6], ACT.Exp, scale=-1.0).then_inc(mid_act, 1)
                e.wait_ge(mid_done, 2)
                e.activation(sdt[:, 4], sdt[:, 2], ACT.Ln).then_inc(mid_act, 1)
                e.wait_ge(mid_done, 3)
                e.activation(trig[:, 0], trig[:, 2], ACT.Sin)
                e.activation(trig[:, 1], trig[:, 3], ACT.Sin, bias=epsc[:, 1:2], scale=-1.0).then_inc(mid_act, 1)
                e.wait_ge(out_dve, taken[first["z"] - 1][1])
                for t in range(TT):
                    o.then(e.activation(gst[:, 0, 0:Q_LORA], mid[:, t, 2 * HEADS:2 * HEADS + Q_LORA], ACT.Square,
                                        accum_out=stat[:, 12 + t:13 + t]))
                    o.then(e.activation(gst[:, 1, 0:KV_LORA], mid[:, t, 2 * HEADS + Q_LORA:2 * HEADS + Q_LORA + KV_LORA],
                                        ACT.Square, accum_out=stat[:, 16 + t:17 + t]))
                o.did(e.activation(stat[:, 20:24], stat[:, 12:16], ACT.Sqrt, bias=epsc[:, 0:1], scale=1.0 / Q_LORA))
                e.activation(stat[:, 24:28], stat[:, 16:20], ACT.Sqrt, bias=epsc[:, 0:1], scale=1.0 / KV_LORA
                             ).then_inc(mid_act, 1)
            if stage == "z" and j == 3:
                e.wait_ge(acs_out, 2)
                e.activation(sdt[:, 4], sdt[:, 2], ACT.Exp).then_inc(acs_exp, 1)
                e.activation(sdt[:, 6], sdt[:, 5], ACT.Exp).then_inc(acs_exp, 1)
                e.activation(sdt[:, 7], ps[:, 6, 128:256].rearrange("p (t h) -> p t h", t=TT), ACT.Exp
                             ).then_inc(acs_exp, 1)
            if stage == "z" and j == 1:
                for k in range(KQ):
                    act_turn(e, "qa", k, qaH[:, k, :], V_QA)
                for k in range(KKV):
                    act_turn(e, "ka", k, kaH[:, k, :], V_KA)

    def act_ssd(e):
        for s, (kind, n) in enumerate(scan):
            if kind == "y":
                c, g, hf = n // 4, n // 2 % 2, n % 2
                e.wait_ge(lr_mm, n + 1)
                wait_if(e, yd_mm, n - 1)
                for d in range(2):
                    for h in range(4):
                        col = d * HEADS + g * HPG + hf * 4 + h
                        ins = e.activation(LM[:, n % 2, d, h, :], ps[:, d, h * P:(h + 1) * P], ACT.Exp,
                                           bias=sdt[:, 3, c, col:col + 1])
                ins.then_inc(lx_exp, 1)
            if s in beside:
                c = beside[s]
                i = c - first["gate"]
                act_hi(e, c + 1)
                e.wait_ge(gemm_done, 2 * (c + 1))
                wait_if(e, g_st[i % 2], 16 * (i // 2))
                e.activation(gst[:, i % 2, :], gate_bank(c), ACT.Copy).then_inc(out_act, 2)
            if kind == "y" and n % 2 == 1 and n >= 3:
                square_y(e, (n - 3) // 2)

    def act_ssd_rest(e):
        square_y(e, 2 * NSC - 1)
        e.wait_ge(ysq, 2 * NSC)
        e.activation(stat[:, 44:52], stat[:, 36:44], ACT.Sqrt, bias=epsc[:, 0:1], scale=1.0 / GD).then_inc(ys_rt, 1)

    def square_y(e, i):
        c, g = i // 2, i % 2
        e.wait_ge(ysum, i + 1)
        wait_if(e, ysq, i)
        e.activation(ya[:, 3, :], ztok[:, c, g * GD:(g + 1) * GD], ACT.Square,
                     accum_out=stat[:, 36 + i:37 + i]).then_inc(ysq, 1)

    def act_gate(e, i):
        e.wait_ge(g_load[i % 2], 16 * (i // 2 + 1))
        e.activation(gld[:, i % 2, :], gld[:, i % 2, :], ACT.Sigmoid).then_inc(g_sig, 1)

    def act_pssd(e):
        for k in range(KD):
            act_turn(e, "ys", k, actH[:, k, :], V_SSD)
        for c in range(first["pssd"], first["pmla"]):
            if c > first["pssd"]:
                act_hi(e, c + 1)
            for m in range(2):
                act_gate(e, 2 * (c - first["pssd"]) + m)
        act_hi(e, first["pmla"] + 1)

    def act_attention(e):
        def queries_out(u):
            c = first["q"] + 2 * u
            if u == 0:
                act_hi(e, c + 1)
            for m in range(2):
                e.wait_ge(gemm_done, 2 * c + m + 1)
                if u >= 1:
                    e.wait_ge(q_tr, 2 * u)
                e.activation(qrot[:, 2 * m:2 * m + 2, :, :], bank_tokens(c, m).rearrange("p t (h n) -> p t h n", h=2),
                             ACT.Copy, scale=SCALE).then_inc(out_act, 1)

        def rest_out(u):
            c = first["q"] + 2 * u + 1
            for h in range(2):
                e.wait_ge(q_tr, 2 * u + h + 1)
                if u >= 2:
                    e.wait_ge(s_mm, 8 * (u - 1))
                e.activation(QT[0:QK, u % 2, h, :], ps[0:QK, turned_bank(h), :], ACT.Copy).then_inc(q_out, 1)
            act_hi(e, c + 1)
            act_hi(e, c + 2)

        queries_out(0)
        rest_out(0)
        for n, (u, h, t) in enumerate(attn):
            if n == 12:
                act_ssd_rest(e)
            if t == 2 and h == 0 and u + 1 < NU:
                queries_out(u + 1)
            if t == 1 and h == 1 and u + 1 < NU:
                rest_out(u + 1)
            e.wait_ge(mx_done, n + 1)
            wait_if(e, p_tr, n - 1)
            e.activation(Pr[:, n % 2, :], ps[:, 4 + n % 2, :], ACT.Exp, bias=nmx[:, n % 4:n % 4 + 1],
                         accum_out=rsum[:, n % 8:n % 8 + 1]).then_inc(e_done, 1)
            if n >= 1:
                copy_p(e, n - 1)
        copy_p(e, len(attn) - 1)

    def copy_p(e, n):
        e.wait_ge(p_tr, n + 1)
        wait_if(e, pv_mm, n - 1)
        e.activation(PT[:, n % 2, :, :], ps[:, 6, :].rearrange("p (k n) -> p k n", k=TT), ACT.Copy).then_inc(p_out, 1)

    def act_merge(e):
        for k in range(KD):
            act_turn(e, "ym", k, actH[:, k, :], None)
        for c in range(first["pmla"], first["out"]):
            if c > first["pmla"]:
                act_hi(e, c + 1)
            for m in range(2):
                i = 2 * (c - first["pmla"]) + m
                act_gate(e, KD + i)
                e.wait_ge(m_sum, i + 1)
                e.activation(mH[:, i, :], mtmp[:, i % 2, :], ACT.Copy).then_inc(m_hi, 1)
        for c in range(first["out"], first["pq"]):
            act_hi(e, c + 1)

    def dve_front(e, o):
        e.wait_ge(x_rt, 1)
        o.then(e.reciprocal(stat[:, 8:12], stat[:, 4:8]))
        for t in range(TT):
            e.tensor_scalar(utok[:, t, :], X[:, t, :], stat[:, 8 + t:9 + t], None, ALU.mult).then_inc(u_tok, 1)
        e.wait_ge(vt_tr, 1)
        e.tensor_copy(vecT[:, 0:NV], ps[:, 6, 0:NV]).then_inc(vt_ready, 1)
        e.wait_ge(mid_act, 1)
        o.did(e.tensor_scalar(aneg[:], sdt[:, 6, 0, :], -1.0, None, ALU.mult))
        o.then(e.tensor_copy(posf[:], posi[:]))
        NF = QK_ROPE // 2
        o.then(e.tensor_tensor(trig[:, 2], posf[:].unsqueeze(2).broadcast_to([P, TT, NF]),
                               inv[:].unsqueeze(1).broadcast_to([P, TT, NF]), ALU.mult))
        big = 1.5 * 2 ** 23
        o.then(e.tensor_scalar(trig[:, 3], trig[:, 2], 1.0 / TWO_PI, big, ALU.mult, ALU.add))
        o.then(e.tensor_scalar(trig[:, 3], trig[:, 3], -big, None, ALU.add))
        c1 = 6.28125
        c2 = float(np.round((TWO_PI - c1) * 2 ** 20) / 2 ** 20)
        c3 = TWO_PI - c1 - c2
        for cc in (c1, c2, c3):
            o.then(e.scalar_tensor_tensor(out=trig[:, 2], in0=trig[:, 3], scalar=-cc, in1=trig[:, 2],
                                          op0=ALU.mult, op1=ALU.add))
        o.then(e.tensor_scalar(trig[:, 2], trig[:, 2], 3.1415925, -3.1415925, ALU.min, ALU.max))
        o.did(e.scalar_tensor_tensor(out=trig[:, 3], in0=trig[:, 2], scalar=-1.0, in1=trig[:, 2], op0=ALU.mult, op1=ALU.max))
        dve_lo(e, 0)
        dve_lo(e, 1)
        for k in range(KD):
            dve_turn(e, "u", k, actH[:, k, :], actL[:, k, :], V_MIX)

        def conv_out(ct):
            e.wait_ge(ct_tr, ct + 1)
            dst = xtok[:, :, ct * P:(ct + 1) * P] if ct < XS_CT else Btok[:, :, (ct - XS_CT) * P:(ct - XS_CT + 1) * P]
            e.tensor_copy(dst, ps[:, 4 + ct % 2, :].rearrange("p (t n) -> p t n", t=TT)).then_inc(ct_out, 1)

        for c, (stage, j, *_) in enumerate(chunks[:first["gate"]]):
            if c > 0:
                dve_lo(e, c + 1)
            if stage == "conv":
                for m in range(2):
                    ct = 2 * j + m
                    e.wait_ge(out_act, taken[c][1] - 1 + m)
                    wait_if(e, cact_done, ct - 1)
                    w = [vecT[:, V_CW + CT_N * r + ct:V_CW + CT_N * r + ct + 1] for r in range(3)]
                    bias = vecT[:, V_CB + ct:V_CB + ct + 1]
                    o.then(e.tensor_scalar(conv[:, m, :], pre[:, m, 0:S], w[0], bias, ALU.mult, ALU.add))
                    o.then(e.scalar_tensor_tensor(out=conv[:, m, :], in0=pre[:, m, 1:S + 1], scalar=w[1],
                                                  in1=conv[:, m, :], op0=ALU.mult, op1=ALU.add))
                    e.scalar_tensor_tensor(out=conv[:, m, :], in0=pre[:, m, 2:S + 2], scalar=w[2],
                                           in1=conv[:, m, :], op0=ALU.mult, op1=ALU.add).then_inc(conv_done, 1)
                if j >= 1:
                    conv_out(2 * j - 2)
                    conv_out(2 * j - 1)
            if stage == "mid":
                for m in range(2):
                    e.wait_ge(gemm_done, 2 * c + m + 1)
                    e.tensor_copy(mid[:, 2 * m:2 * m + 2, j * 256:j * 256 + chunks[c][4]], bank_tokens(c, m)).then_inc(out_dve, 1)
            if stage == "mid" and c == first["z"] - 1:
                e.wait_ge(out_dve, taken[c][1])
                o.then(e.tensor_tensor(sdt[:, 5], mid[:, :, 0:2 * HEADS],
                                       dtb[:].unsqueeze(1).broadcast_to([P, TT, 2 * HEADS]), ALU.add))
                e.scalar_tensor_tensor(out=sdt[:, 6], in0=sdt[:, 5], scalar=-1.0, in1=sdt[:, 5], op0=ALU.mult, op1=ALU.max).then_inc(mid_done, 1)
            if stage == "z" and j == 0:
                e.wait_ge(mid_act, 2)
                e.tensor_scalar(sdt[:, 2], sdt[:, 7], 1.0, None, ALU.add).then_inc(mid_done, 1)
                e.wait_ge(dvo, o.n)
                e.wait_ge(mid_done, 2)
                o.then(e.tensor_scalar(sdt[:, 3], sdt[:, 2], -1.0, 1e-37, ALU.add, ALU.max))
                e.reciprocal(sdt[:, 3], sdt[:, 3]).then_inc(mid_done, 1)
                e.wait_ge(mid_done, 3)
                e.wait_ge(mid_act, 3)
                o.then(e.tensor_tensor(sdt[:, 6], sdt[:, 4], sdt[:, 7], ALU.mult))
                o.then(e.tensor_tensor(sdt[:, 6], sdt[:, 6], sdt[:, 3], ALU.mult))
                o.then(e.scalar_tensor_tensor(out=sdt[:, 0], in0=sdt[:, 5], scalar=0.0, in1=sdt[:, 6],
                                              op0=ALU.max, op1=ALU.add))
                e.tensor_tensor(sdt[:, 1], sdt[:, 0], aneg[:].unsqueeze(1).broadcast_to([P, TT, 2 * HEADS]),
                                ALU.mult).then_inc(a_ready, 1)
            if stage == "z" and j == 0:
                e.wait_ge(mid_act, 5)
                o.then(e.reciprocal(stat[:, 28:36], stat[:, 20:28]))
                for t in range(TT):
                    q0 = 2 * HEADS
                    e.tensor_scalar(mid[:, t, q0:q0 + Q_LORA], mid[:, t, q0:q0 + Q_LORA], stat[:, 28 + t:29 + t],
                                    None, ALU.mult).then_inc(qk_tok, 1)
                    q0 += Q_LORA
                    e.tensor_scalar(mid[:, t, q0:q0 + KV_LORA], mid[:, t, q0:q0 + KV_LORA], stat[:, 32 + t:33 + t],
                                    None, ALU.mult).then_inc(qk_tok, 1)
                r0 = MID - QK_ROPE
                x1, x2 = mid[:, :, r0:r0 + NF], mid[:, :, r0 + NF:r0 + 2 * NF]
                o.did(e.tensor_tensor(trig[:, 2], x1, trig[:, 1], ALU.mult))
                o.did(e.tensor_tensor(trig[:, 3], x2, trig[:, 0], ALU.mult))
                o.did(e.tensor_tensor(trig[:, 4], x1, trig[:, 0], ALU.mult))
                o.then(e.tensor_tensor(trig[:, 5], x2, trig[:, 1], ALU.mult))
                e.tensor_tensor(krot[:, :, QK_NOPE:QK_NOPE + NF], trig[:, 2], trig[:, 3], ALU.subtract).then_inc(qk_tok, 1)
                e.tensor_tensor(krot[:, :, QK_NOPE + NF:QK], trig[:, 4], trig[:, 5], ALU.add).then_inc(qk_tok, 1)
            if stage == "z" and j == 3:
                e.wait_ge(acs_mm, 1)
                o.did(e.tensor_copy(sdt[:, 2, :, 0:HEADS], ps[:, 6, 0:64].rearrange("p (t h) -> p t h", t=TT)))
                o.then(e.tensor_copy(sdt[:, 2, :, HEADS:2 * HEADS], ps[:, 6, 64:128].rearrange("p (t h) -> p t h", t=TT)))
                e.tensor_scalar(sdt[:, 3], sdt[:, 2], -1.0, None, ALU.mult).then_inc(acs_out, 1)
                e.tensor_tensor(sdt[:, 5], ps[:, 6, 128:256].rearrange("p (t h) -> p t h", t=TT), sdt[:, 2],
                                ALU.subtract).then_inc(acs_out, 1)
            if stage == "z" and j == 3:
                e.wait_ge(acs_exp, 3)
                o.then(e.tensor_tensor(sdt[:, 5], sdt[:, 0], sdt[:, 6], ALU.mult))
            if stage == "z" and j == 1:
                e.wait_ge(kr_tr, 1)
                e.tensor_copy(kropeT[QK_NOPE:QK, :], ps[QK_NOPE:QK, 7, :]).then_inc(kr_out, 1)
                for k in range(KQ):
                    dve_turn(e, "qa", k, qaH[:, k, :], qaL[:, k, :], V_QA)
                for k in range(KKV):
                    dve_turn(e, "ka", k, kaH[:, k, :], kaL[:, k, :], V_KA)

    def dve_ssd(e, o):
        e.wait_ge(gemm_done, 2 * first["gate"])

        def fac(k, c, d):
            return over(sdt[:, k, c, d * HEADS:(d + 1) * HEADS], HD)

        def decayed(i):
            wait_if(e, st_mm, 4 * i)
            for d in range(2):
                c = i if d == 0 else NSC - 1 - i
                e.tensor_tensor(heads(xdec[:, d, :]), heads(xtok[:, c, :]), fac(5, c, d), ALU.mult).then_inc(xdec_ready, 1)

        def states_out(i):
            for d in range(2):
                c = i if d == 0 else NSC - 1 - i
                for g in range(N_GROUPS):
                    n = 4 * i + 2 * d + g
                    dst = prev[:, d, g, i, :]
                    if i == 0:
                        e.wait_ge(st_mm, n + 1)
                        e.tensor_copy(dst, ps[:, 6 + n % 2, :]).then_inc(st_out, 1)
                        continue
                    e.wait_ge(st_out, 4 * i)
                    dec = over(sdt[:, 7, c, d * HEADS + g * HPG:d * HEADS + (g + 1) * HPG], HD)
                    o.then(e.tensor_tensor(heads(dst), heads(prev[:, d, g, i - 1, :]), dec, ALU.mult))
                    e.wait_ge(st_mm, n + 1)
                    e.tensor_tensor(dst, ps[:, 6 + n % 2, :], dst, ALU.add).then_inc(st_out, 1)

        def weights(n):
            c, g = n // 4, n // 2 % 2
            if n % 4 == 0:
                wait_if(e, yd_mm, n)
                for d in range(2):
                    e.tensor_tensor(heads(xd[:, d, :]), heads(xtok[:, c, :]), fac(0, c, d), ALU.mult).then_inc(xd_ready, 1)
            e.wait_ge(lx_exp, n + 1)
            lm = LM[:, n % 2].rearrange("p d h n -> p (d h) n")
            e.tensor_tensor(lm, lm, CB[:, c, g, :].unsqueeze(1).broadcast_to([P, 8, P]), ALU.mult).then_inc(m_done, 1)

        def group_out(c, g):
            gs = slice(g * GD, (g + 1) * GD)
            hs = slice(g * HPG, (g + 1) * HPG)
            wait_if(e, ysum, 2 * c + g)
            o.did(e.tensor_tensor(heads(ya[:, 0, :]), heads(xtok[:, c, gs]), over(dsk[:, hs], HD), ALU.mult))
            e.wait_ge(yo_mm, 2 * c + g + 1)
            if c > 0:
                o.did(e.tensor_tensor(heads(ya[:, 1, :]), heads(ps[:, 7, :]), over(sdt[:, 4, c, hs], HD), ALU.mult))
            if c < NSC - 1:
                o.did(e.tensor_tensor(heads(ya[:, 2, :]), heads(ps[:, 6, :]),
                                      over(sdt[:, 4, c, HEADS + g * HPG:HEADS + (g + 1) * HPG], HD), ALU.mult))
            o.wait()
            o.then(e.tensor_tensor(ya[:, 0, :], ps[:, 4 + g, :], ya[:, 0, :], ALU.add))
            if c > 0:
                o.then(e.tensor_tensor(ya[:, 0, :], ya[:, 0, :], ya[:, 1, :], ALU.add))
            if c < NSC - 1:
                o.then(e.tensor_tensor(ya[:, 0, :], ya[:, 0, :], ya[:, 2, :], ALU.add))
            e.tensor_tensor(ztok[:, c, gs], ya[:, 0, :], ztok[:, c, gs], ALU.mult).then_inc(ysum, 1)

        for s, (kind, n) in enumerate(scan):
            if kind == "state":
                decayed(n)
            else:
                weights(n)
            if s in beside:
                dve_lo(e, beside[s] + 1)
            if s == 0:
                e.wait_ge(cb_mm, 1)
                e.tensor_copy(CB[:].rearrange("p c g n -> p (c g n)"), ps[:, 4:6, :].rearrange("p b n -> p (b n)")
                              ).then_inc(cb_out, 1)
                e.wait_ge(cb_out, 1)
            if kind == "state":
                states_out(n)
            elif n % 2 == 1:
                group_out(n // 4, n // 2 % 2)

    def dve_ssd_rest(e, o):
        e.wait_ge(ysum, 2 * NSC)
        e.wait_ge(ys_rt, 1)
        o.then(e.reciprocal(stat[:, 52:60], stat[:, 44:52]))
        for i in range(2 * NSC):
            c, g = i // 2, i % 2
            gs = slice(g * GD, (g + 1) * GD)
            e.tensor_scalar(ztok[:, c, gs], ztok[:, c, gs], stat[:, 52 + i:53 + i], None, ALU.mult).then_inc(ys_tok, 1)

    def gated(e, c, m, base):
        i = base + 2 * (c - first["pssd" if base == 0 else "pmla"]) + m
        e.wait_ge(g_sig, i + 1)
        e.wait_ge(gemm_done, 2 * c + m + 1)
        return i

    def dve_pssd(e):
        for k in range(KD):
            dve_turn(e, "ys", k, actH[:, k, :], actL[:, k, :], V_SSD)
        for c in range(first["pssd"], first["pmla"]):
            if c > first["pssd"]:
                dve_lo(e, c + 1)
            for m in range(2):
                i = gated(e, c, m, 0)
                e.tensor_tensor(mS[:, i, :], bank(c, m), gld[:, i % 2, :], ALU.mult).then_inc(out_dve, 1)

    def dve_attention(e, o):
        NF = QK_ROPE // 2
        for s in range(2):
            for h in range(2):
                o.did(e.tensor_copy(KT[QK_NOPE:QK, s, h, :], kropeT[QK_NOPE:QK, :]))
        o.wait()

        def rotate(u):
            c = first["q"] + 2 * u
            if u == 0:
                dve_lo(e, c + 1)
            e.wait_ge(out_act, taken[c][1])
            x1 = qrot[:, :, :, QK_NOPE:QK_NOPE + NF]
            x2 = qrot[:, :, :, QK_NOPE + NF:QK]
            sin = trig[:, 0].unsqueeze(2).broadcast_to([P, TT, 2, NF])
            cos = trig[:, 1].unsqueeze(2).broadcast_to([P, TT, 2, NF])
            o.did(e.tensor_tensor(rtmp[:, 0], x1, cos, ALU.mult))
            o.did(e.tensor_tensor(rtmp[:, 1], x2, sin, ALU.mult))
            o.did(e.tensor_tensor(rtmp[:, 2], x1, sin, ALU.mult))
            o.then(e.tensor_tensor(rtmp[:, 3], x2, cos, ALU.mult))
            e.tensor_tensor(x1, rtmp[:, 0], rtmp[:, 1], ALU.subtract).then_inc(qrot_done, 1)
            e.tensor_tensor(x2, rtmp[:, 2], rtmp[:, 3], ALU.add).then_inc(qrot_done, 1)
            c += 1
            for h in range(2):
                e.wait_ge(gemm_done, 2 * c + h + 1)
                if u >= 2:
                    e.wait_ge(s_mm, 8 * (u - 1))
                e.tensor_copy(KT[0:QK_NOPE, u % 2, h, :], bank(c, h)[0:QK_NOPE, :]).then_inc(out_dve, 1)

        def values_out(u):
            c = first["q"] + 2 * u + 1
            e.wait_ge(v_done, u + 1)
            if u >= 2:
                e.wait_ge(pv_mm, 8 * (u - 1))
            e.tensor_copy(Vt[:, u % 2].rearrange("p t h n -> p (t h n)"), ps[:, QA_BANK, :]).then_inc(v_out, 1)
            dve_lo(e, c + 1)
            dve_lo(e, c + 2)

        def row_max(n):
            e.wait_ge(s_mm, n + 1)
            wait_if(e, e_done, n - 3)
            e.tensor_reduce(nmx[:, n % 4:n % 4 + 1], ps[:, 4 + n % 2, :], AX_X, ALU.max, negate=True).then_inc(mx_done, 1)

        def head_out(hh):
            e.wait_ge(e_done, TT * (hh + 1))
            o.then(e.reciprocal(rsum[:, 8:12], rsum[:, hh % 2 * TT:hh % 2 * TT + TT]))
            e.wait_ge(pv_mm, TT * (hh + 1))
            e.tensor_tensor(ytok[:, :, hh * V_HEAD:(hh + 1) * V_HEAD],
                            ps[:, 7, 0:TT * V_HEAD].rearrange("p (t n) -> p t n", t=TT),
                            rsum[:, 8:12].unsqueeze(2).broadcast_to([P, TT, V_HEAD]), ALU.mult).then_inc(y_done, 1)

        rotate(0)
        values_out(0)
        row_max(0)
        for n, (u, h, t) in enumerate(attn):
            if t == 1 and n > TT:
                head_out(n // TT - 1)
            if n + 1 < len(attn):
                row_max(n + 1)
            if n == 16:
                dve_ssd_rest(e, o)
            if t == 2 and h == 0 and u + 1 < NU:
                rotate(u + 1)
            if t == 1 and h == 1 and u + 1 < NU:
                values_out(u + 1)
        head_out(A_HEADS - 1)

    def dve_merge(e):
        dve_lo(e, first["pmla"] + 1)
        for k in range(KD):
            dve_turn(e, "ym", k, actH[:, k, :], actL[:, k, :], None)
        for c in range(first["pmla"], first["out"]):
            if c > first["pmla"]:
                dve_lo(e, c + 1)
            for m in range(2):
                i = gated(e, c, m, KD)
                ct = i - KD
                wait_if(e, m_lo, ct - 1)
                e.tensor_tensor(mtmp[:, i % 2, :], bank(c, m), gld[:, i % 2, :], ALU.mult).then_inc(out_dve, 1)
                e.wait_ge(out_dve, taken[c][1] - 1 + m)
                e.tensor_tensor(mtmp[:, i % 2, :], mtmp[:, i % 2, :], mS[:, ct, :], ALU.add).then_inc(m_sum, 1)
                e.wait_ge(m_hi, ct + 1)
                e.tensor_tensor(mL[:, ct, :], mtmp[:, i % 2, :], mH[:, ct, :].bitcast(F32), ALU.subtract).then_inc(m_lo, 1)
        for c in range(first["out"], first["pq"]):
            dve_lo(e, c + 1)
            j = c - first["out"]
            for m in range(2):
                e.wait_ge(gemm_done, 2 * c + m + 1)
                dst = X[:, 2 * m:2 * m + 2, j * 256:(j + 1) * 256]
                e.tensor_tensor(dst, bank_tokens(c, m), dst, ALU.add).then_inc(out_dve, 1)


    h_sq, h_rt = sem("h_sq"), sem("h_rt")
    u2_tok = sem("u2_tok")
    sk_in, sk_tr, sk_out = sem("sk_in"), sem("sk_tr"), sem("sk_out")
    sc_mm = sem("sc_mm")
    sc_out = sem("sc_out")
    g_shift, g_exp = sem("g_shift"), sem("g_exp")
    r_done, r_tr, r_out = sem("r_done"), sem("r_tr"), sem("r_out")
    ohe_done = sem("ohe_done")
    oh_done = sem("oh_done")
    ohp_done = sem("ohp_done")
    gq_mm = sem("gq_mm")
    gq_out = sem("gq_out")
    gb_st = [sem(f"gb_st{s}") for s in range(2)]
    u_in = [sem(f"u_in{s}") for s in range(4)]
    ga_st = [sem(f"ga_st{s}") for s in range(4)]
    v_in = [sem(f"v_in{s}") for s in range(4)]
    hid_in = [sem(f"hid_in{s}") for s in range(4)]
    gt_in = [sem(f"gt_in{s}") for s in range(2)]
    wf_in = sem("wf_in")
    t_mm = sem("t_mm")
    t_hi = sem("t_hi")
    t_lo = sem("t_lo")
    h_mm = sem("h_mm")
    h_gelu = sem("h_gelu")
    w_mul = sem("w_mul")
    wt_hi = sem("wt_hi")
    wt_lo = sem("wt_lo")
    vt_hi = sem("vt_hi")
    vt_lo = sem("vt_lo")
    o_mm = sem("o_mm")
    o_add = sem("o_add")
    f_sq, f_rt, f_out, f_st = sem("f_sq"), sem("f_rt"), sem("f_out"), sem("f_st")

    NPQ = first["pq"]
    E_TILES = peer_u.shape[0] // P
    NITER = E_TILES // (2 * GRP)
    QPB = TB // 4

    def pe_routing(e):
        e.wait_ge(sk_in, 16)
        for i in range(2):
            ins = e.transpose(ps[:, 6, i * P:(i + 1) * P], skraw[:, i, :], ident[:])
        ins.then_inc(sk_tr, 1)
        e.wait_ge(u2_tok, TT)
        pe_turn_channels(e, "u2", NPQ, lambda k: lambda t: u2tok[:, t, k * P:(k + 1) * P])

        def scores(c, m):
            s = 2 * (c - NPQ) + m
            e.wait_ge(out_act, taken[c][1] - 1 + m)
            wait_if(e, sc_out, s - 1)
            for t in range(TT):
                ins = e.matmul(ps[:, 4 + s % 2, t * P:(t + 1) * P], qT[:, m, t * P:(t + 1) * P], skT[:, s % 2, :],
                               start=True, stop=True)
            ins.then_inc(sc_mm, 1)

        e.wait_ge(sk_out, 1)
        for c in range(NPQ + 1, NCH):
            pe_channels(e, c, actH[:], actL[:])
            scores(c - 1, 0)
            scores(c - 1, 1)
        scores(NCH - 1, 0)
        scores(NCH - 1, 1)

    def act_routing(e):
        for t in range(TT):
            e.wait_ge(out_dve, taken[NPQ - 1][1])
            wait_if(e, h_sq, t)
            if t == 0:
                e.wait_ge(ts_tr, TS["ym"] + KD)
            e.activation(u2tok[:, t, :], X[:, t, :], ACT.Square, accum_out=stat[:, t:t + 1]).then_inc(h_sq, 1)
        e.wait_ge(h_sq, TT)
        e.activation(stat[:, 4:8], stat[:, 0:4], ACT.Sqrt, bias=epsc[:, 0:1], scale=1.0 / D).then_inc(h_rt, 1)
        act_hi(e, NPQ + 1)
        for k in range(KD):
            act_turn(e, "u2", k, actH[:, k, :], V_FFN)
        for c in range(NPQ, NCH):
            if c > NPQ:
                act_hi(e, c + 1)
            for m in range(2):
                e.wait_ge(gemm_done, 2 * c + m + 1)
                if c > NPQ:
                    e.wait_ge(sc_mm, 2 * (c - NPQ) + m - 1)
                e.activation(qT[:, m, :], bank(c, m), ACT.Copy).then_inc(out_act, 1)

    def dve_routing(e, o):
        e.wait_ge(h_rt, 1)
        o.then(e.reciprocal(stat[:, 8:12], stat[:, 4:8]))
        for t in range(TT):
            e.tensor_scalar(u2tok[:, t, :], X[:, t, :], stat[:, 8 + t:9 + t], None, ALU.mult).then_inc(u2_tok, 1)
        dve_lo(e, NPQ + 1)
        for k in range(KD):
            dve_turn(e, "u2", k, actH[:, k, :], actL[:, k, :], V_FFN)
        e.wait_ge(sk_tr, 1)
        e.tensor_copy(skT[:].rearrange("p i n -> p (i n)"), ps[:, 6, 0:2 * P]).then_inc(sk_out, 1)

        def scores_out(s):
            e.wait_ge(sc_mm, s + 1)
            e.tensor_copy(sc[:, :, s, :], ps[:, 4 + s % 2, :].rearrange("p (t n) -> p t n", t=TT)).then_inc(sc_out, 1)

        for c in range(NPQ, NCH):
            if c > NPQ:
                dve_lo(e, c + 1)
            if c > NPQ:
                scores_out(2 * (c - NPQ) - 2)
                scores_out(2 * (c - NPQ) - 1)
        scores_out(2 * P_HEADS - 2)
        scores_out(2 * P_HEADS - 1)
        e.wait_ge(sc_out, 2 * P_HEADS)

    def route(e, o, t):

        def ready():
            o.wait()
            e.tensor_copy(epsc[:, 2:3], epsc[:, 1:2])

        def top16(n, src, rest, vals, idx, cost):
            ready()
            for s in range(n):
                o.did(e.max(vals(s, 0), src(s)))
                yield cost
            ready()
            for s in range(n):
                o.did(e.max_index(idx(s, 0), vals(s, 0), src(s)))
                yield cost
                o.did(e.match_replace(rest(s), vals(s, 0), src(s), NEG))
                yield cost
            ready()
            for s in range(n):
                o.did(e.max(vals(s, 8), rest(s)))
                yield cost
            ready()
            for s in range(n):
                o.did(e.max_index(idx(s, 8), vals(s, 8), rest(s)))
                yield cost
            ready()

        H8 = P_HEADS
        o.did(e.tensor_copy(scur[:], sc[:, bass.ds(t, 1)].rearrange("p a s n -> p (a s) n")))
        yield 1.2
        yield from top16(2 * H8, lambda s: scur[:, s, :], lambda s: cur[:, s, :],
                         lambda s, k: topv[:, s, k:k + 8], lambda s, k: topi[:, s, k:k + 8], 0.2)
        o.did(e.tensor_copy(topf[:], topi[:]))
        yield 0.3
        tv = topv[:].rearrange("p (h i) k -> p h i k", i=2)
        tf = topf[:].rearrange("p (h i) k -> p h i k", i=2)
        grid = [P, H8, TOPK, TOPK]
        o.wait()
        o.did(e.tensor_tensor(cand[:].rearrange("p h (a b) -> p h a b", a=TOPK),
                               tv[:, :, 0, :].unsqueeze(3).broadcast_to(grid),
                               tv[:, :, 1, :].unsqueeze(2).broadcast_to(grid), ALU.add))
        yield 2.2
        yield from top16(H8, lambda s: cand[:, s, :], lambda s: cand2[:, s, :],
                         lambda s, k: best[:, s, k:k + 8], lambda s, k: bpos[:, s, k:k + 8], 0.33)
        e.tensor_tensor(gate[:, 0], best[:], best[:, :, 0:1].broadcast_to([P, H8, TOPK]), ALU.subtract
                        ).then_inc(g_shift, 1)
        o.did(e.tensor_scalar(bab[:, 0], bpos[:], 4, None, ALU.logical_shift_right))
        o.then(e.tensor_scalar(bab[:, 1], bpos[:], TOPK - 1, None, ALU.bitwise_and))
        o.then(e.tensor_copy(babf[:], bab[:]))
        yield 0.8
        k16 = iota[:, 0:TOPK].unsqueeze(1).unsqueeze(1).broadcast_to(grid)
        wait_if(e, r_tr, t)
        for i in range(2):
            eq = (cur, pick)[i][:].rearrange("p s (r k) -> p (s r) k", k=TOPK).rearrange("p (h r) k -> p h r k", h=H8)
            o.then(e.tensor_tensor(eq, babf[:, i].unsqueeze(3).broadcast_to(grid), k16, ALU.is_equal))
            yield 2.2
            o.then(e.tensor_tensor(eq, eq, tf[:, :, i, :].unsqueeze(2).broadcast_to(grid), ALU.mult))
            yield 2.2
            e.tensor_reduce(R3[:, i, :].rearrange("p (h r) -> p h r", h=H8), eq, AX_X, ALU.add).then_inc(r_done, 1)
            yield 2.2
        e.wait_ge(g_exp, t + 1)
        o.then(e.tensor_reduce(gsum[:, 0], gate[:, 1], AX_X, ALU.add))
        o.then(e.reciprocal(gsum[:, 1], gsum[:, 0]))
        e.tensor_tensor(R3[:, 2, :].rearrange("p (h r) -> p h r", h=H8), gate[:, 1],
                        gsum[:, 1].unsqueeze(2).broadcast_to([P, H8, TOPK]), ALU.mult).then_inc(r_done, 1)
        yield 0.6

    def pe_route(e, t):
        e.wait_ge(r_done, 3 * t + 3)
        wait_if(e, r_out, t)
        for r in range(3):
            ins = e.transpose(ps[:, 6, r * P:(r + 1) * P], R3[:, r, :], ident[:])
        ins.then_inc(r_tr, 1)

    def act_route(e, t):
        e.wait_ge(g_shift, t + 1)
        e.activation(gate[:, 1], gate[:, 0], ACT.Exp).then_inc(g_exp, 1)

    def dve_route_out(e, t):
        e.wait_ge(r_tr, t + 1)
        e.tensor_copy(rt[:, :, bass.ds(t * P, P)], ps[:, 6, 0:3 * P].rearrange("p (r n) -> p r n", r=3)
                      ).then_inc(r_out, 1)

    def dve_onehots(e, b2, q):
        n = b2 * 2 * QPB + q
        toks = bass.ds(n * 4, 4)
        numbers = iotab[:].unsqueeze(1).broadcast_to([P, 4, P])
        wait_if(e, gq_mm, n - 1)
        e.tensor_tensor(oneE[:, q % 2], numbers, ib16[:, toks].unsqueeze(2).broadcast_to([P, 4, P]), ALU.is_equal
                        ).then_inc(ohe_done, 1)
        e.tensor_tensor(oneJ[:, q % 2], numbers, jb16[:, toks].unsqueeze(2).broadcast_to([P, 4, P]), ALU.is_equal)
        e.wait_ge(ohe_done, n + 1)
        e.tensor_tensor(oneI[:, q % 2, 0], oneE[:, q % 2], rt[:, 2, toks].unsqueeze(2).broadcast_to([P, 4, P]), ALU.mult
                        ).then_inc(oh_done, 1)

    def pool_onehots(e, b2, q):
        n = b2 * 2 * QPB + q
        e.wait_ge(ohe_done, n + 1)
        for k, rest in ((1, rest1), (2, rest2)):
            ins = e.tensor_tensor(oneI[:, q % 2, k], oneE[:, q % 2],
                                  rest[:, bass.ds(n * 4, 4)].unsqueeze(2).broadcast_to([P, 4, P]), ALU.mult)
        ins.then_inc(ohp_done, 1)

    def pe_gates(e, b2, q):
        n = b2 * 2 * QPB + q
        e.wait_ge(oh_done, n + 1)
        e.wait_ge(ohp_done, n + 1)
        wait_if(e, gq_out, n - 1)
        for r in range(4):
            for k in range(3):
                ins = e.matmul(ps[:, 6 + q % 2, r * P:(r + 1) * P], oneJ[:, q % 2, r, :], oneI[:, q % 2, k, r, :],
                               start=k == 0, stop=k == 2)
        ins.then_inc(gq_mm, 1)

    def act_gates(e, b2, q):
        n = b2 * 2 * QPB + q
        s, qq = q // QPB, q % QPB
        if qq == 0:
            wait_if(e, gb_st[s], 16 * b2)
        e.wait_ge(gq_mm, n + 1)
        e.activation(Gst[:, s, :, 4 * qq:4 * qq + 4].rearrange("p i t -> p t i"),
                     ps[:, 6 + q % 2, :].rearrange("p (t i) -> p t i", t=4), ACT.Copy).then_inc(gq_out, 1)

    def pool_gates(e, b2):
        def store(b, s):
            e.wait_ge(gq_out, b * QPB + QPB)
            e.dma_start(G_dram[bass.ds(b, 1)].rearrange("b j i t -> j (b i t)"),
                        Gst[:, s].rearrange("p i t -> p (i t)")).then_inc(gb_st[s], 16)

        for q in range(2 * QPB):
            pool_onehots(e, b2, q)
            if q == 2 and not (isinstance(b2, int) and b2 == 0):
                store(b2 * 2 - 1, 1)
            if q == QPB + 2:
                store(b2 * 2, 0)

    def in_slot(e, sems, E, x):
        e.wait_ge(sems[x], 4 * E + 16 - 4 * x)

    def pe_turn_u(e, E, x):
        in_slot(e, u_in, E, x)
        wait_if(e, t_lo, 2 * E - 2)
        for hf in range(2):
            for k in range(4):
                ins = e.transpose(ps[:, 2 + 2 * (x % 2) + hf, k * P:(k + 1) * P],
                                  Uraw[:, x, (4 * hf + k) * P:(4 * hf + k + 1) * P], ident[:])
            ins.then_inc(t_mm, 1)

    def pe_hidden(e, E, x, turn=True):
        e.wait_ge(t_lo, 2 * E + 2)
        wait_if(e, h_gelu, E - 1)
        product3(e, ps[:, x % 2, :], [(UTh[:, x % 2, k, :], UTl[:, x % 2, k, :], actH[:, k, :], actL[:, k, :])
                                      for k in range(KD)]).then_inc(h_mm, 1)
        if turn:
            pe_turn_u(e, E + 2, (x + 2) % 4)

    def act_turn_u(e, E, x):
        wait_if(e, h_mm, E - 1)
        for hf in range(2):
            e.wait_ge(t_mm, 2 * E + hf + 1)
            e.activation(UTh[:, x % 2, 4 * hf:4 * hf + 4, :], ps[:, 2 + 2 * (x % 2) + hf, :].rearrange("p (k n) -> p k n", k=4),
                         ACT.Copy).then_inc(t_hi, 1)

    def act_hidden(e, E, x, turn=True):
        e.wait_ge(h_mm, E + 1)
        if not (isinstance(E, int) and E < 4):
            e.wait_ge(ga_st[x], 4 * E - 4 * x)
        e.activation(ga[:, x, :], ps[:, x % 2, :], ACT.Gelu).then_inc(h_gelu, 1)
        if turn:
            act_turn_u(e, E + 2, (x + 2) % 4)

    def dve_turn_u(e, E, x):
        for hf in range(2):
            e.wait_ge(t_hi, 2 * E + hf + 1)
            e.tensor_tensor(UTl[:, x % 2, 4 * hf:4 * hf + 4, :],
                            ps[:, 2 + 2 * (x % 2) + hf, :].rearrange("p (k n) -> p k n", k=4),
                            UTh[:, x % 2, 4 * hf:4 * hf + 4, :].bitcast(F32), ALU.subtract).then_inc(t_lo, 1)

    def dve_hidden(e, E, x, turn=True):
        if turn:
            dve_turn_u(e, E + 2, (x + 2) % 4)

    def sp_load_u(e, E, x):
        e.dma_start(Uraw[:, x, :], peer_u[bass.ds(E * P, P), :]).then_inc(u_in[x], 16)

    def sp_hidden(e, E, x, load=True):
        e.wait_ge(h_gelu, E + 1)
        e.dma_start(act_dram[bass.ds(E, 1)].rearrange("a j t -> j (a t)"), ga[:, x, :]).then_inc(ga_st[x], 16)
        if load:
            e.wait_ge(t_mm, 2 * E + 6)
            sp_load_u(e, E + 6, (x + 2) % 4)

    R_TILES, L_TILES, G_TILES = 12, 4, 8
    R_END = TT * R_TILES
    G0 = R_END + L_TILES
    G_END = G0 + (NTB // 2) * G_TILES
    assert G_END + 2 <= E_TILES and R_TILES % 4 == L_TILES % 4 == G_TILES % 4 == 0

    def sp_second(e, E, x):
        g = x // GRP
        if x % GRP == 0:
            wait_if(e, w_mul, E - GRP)
            e.dma_start(Gt[:, g].rearrange("p b i t -> p b (i t)"),
                        G_dram[:, :, bass.ds(E, GRP), :].rearrange("b j i t -> j b (i t)")).then_inc(gt_in[g], 16)
        wait_if(e, w_mul, E - 3)
        e.dma_start(hid[:, x % 4, :], act_dram[bass.ds(E, 1)].rearrange("a j t -> j (a t)")).then_inc(hid_in[x % 4], 16)

    def pool_second(e, E, x):
        wait_if(e, vt_lo, E - 3)
        e.dma_start(Vraw[:, x % 4, :], peer_v[bass.ds(E * P, P), :]).then_inc(v_in[x % 4], 16)

    def act_second(e, E, x):
        g, k = x // GRP, x % GRP
        in_slot(e, v_in, E, x % 4)
        if isinstance(E, int) and E == GRP:
            e.wait_ge(h_mm, E_TILES)
        wait_if(e, o_mm, 2 * (E - k) - 8)
        e.activation(Vh[g][:, k, :], Vraw[:, x % 4, :], ACT.Copy).then_inc(vt_hi, 1)
        e.wait_ge(w_mul, E + 1)
        e.activation(Wh[g][:, k, :], Wf[:, x % 2, :], ACT.Copy).then_inc(wt_hi, 1)

    def dve_second(e, E, x):
        g, k = x // GRP, x % GRP
        if k == 0:
            e.wait_ge(gt_in[g], 2 * (E - x) + 16)
        in_slot(e, hid_in, E, x % 4)
        wait_if(e, wt_lo, E - 1)
        e.tensor_tensor(Wf[:, x % 2, :].rearrange("p (b t) -> p b t", b=NTB),
                        hid[:, x % 4, :].rearrange("p (b t) -> p b t", b=NTB), Gt[:, g, :, k, :], ALU.mult
                        ).then_inc(w_mul, 1)
        e.wait_ge(vt_hi, E + 1)
        e.tensor_tensor(Vl[g][:, k, :], Vraw[:, x % 4, :], Vh[g][:, k, :].bitcast(F32), ALU.subtract
                        ).then_inc(vt_lo, 1)
        e.wait_ge(wt_hi, E + 1)
        e.tensor_tensor(Wl[g][:, k, :], Wf[:, x % 2, :], Wh[g][:, k, :].bitcast(F32), ALU.subtract
                        ).then_inc(wt_lo, 1)
        for b in (2 * k - 2, 2 * k - 1):
            dve_add_output(e, 2 * (E - k) - 8 + b, b % 8)

    def dve_add_output(e, n, b):
        if isinstance(n, int) and n < 0:
            return
        t, hf = b // 2, b % 2
        e.wait_ge(o_mm, n + 1)
        dst = X[:, t, hf * 512:(hf + 1) * 512]
        e.tensor_tensor(dst, ps[:, b, :], dst, ALU.add).then_inc(o_add, 1)

    def pe_second(e, E, g):
        e.wait_ge(wt_lo, E + GRP)
        e.wait_ge(vt_lo, E + GRP)
        for b in range(2 * TT):
            t, hf = b // 2, b % 2
            wait_if(e, o_add, 2 * E + b - 7)
            ts, cs = slice(t * P, (t + 1) * P), slice(hf * 512, (hf + 1) * 512)
            product3(e, ps[:, b, :], [(Wh[g][:, k, ts], Wl[g][:, k, ts], Vh[g][:, k, cs], Vl[g][:, k, cs])
                                      for k in range(GRP)]).then_inc(o_mm, 1)

    EARLY = G_END + 4
    assert EARLY + GRP <= E_TILES

    def early(E):
        return E - EARLY if EARLY <= E < EARLY + GRP else None

    def groups(e, step):
        for x in range(GRP, 8):
            step(e, x, x)
        with e.Fori(1, NITER) as it:
            for x in range(8):
                step(e, it * 8 + x, x)

    with nc.Block() as block:
        @block.sync
        def _(e):
            sp_front(e)
            e.wait_ge(w_lo, NCH)
            for E in range(4):
                sp_load_u(e, E, E)
            e.wait_ge(t_mm, 4)
            sp_load_u(e, 4, 0)
            sp_load_u(e, 5, 1)
            with e.Fori(0, (E_TILES - 8) // 4) as i:
                for x in range(4):
                    sp_hidden(e, i * 4 + x, x)
            for E in range(E_TILES - 8, E_TILES):
                sp_hidden(e, E, E % 4, load=E + 6 < E_TILES)
                if E == E_TILES - 8:
                    e.wait_ge(gb_st[0], 16 * NTB // 2)
                    e.wait_ge(gb_st[1], 16 * NTB // 2)
                if E < E_TILES - 8 + GRP:
                    sp_second(e, E - E_TILES + 8, E - E_TILES + 8)
            for x in range(4):
                e.wait_ge(ga_st[x], 4 * E_TILES)
            groups(e, sp_second)
            for t in range(TT):
                e.wait_ge(f_out, t + 1)
                e.dma_start(out[0, t * P:(t + 1) * P, :], ost[:, t, :]).then_inc(f_st, 16)
            e.wait_ge(f_st, 16 * TT)

        @block.gpsimd
        def _(e):
            pool_front(e)
            e.wait_ge(v_done, NU)
            e.dma_start(skraw[:], peer_sub_keys.rearrange("i n d -> n i d")).then_inc(sk_in, 16)
            pool_gates(e, 0)
            with e.Fori(1, NTB // 2) as b2:
                pool_gates(e, b2)
            e.wait_ge(gq_out, NTB * QPB)
            e.dma_start(G_dram[NTB - 1].rearrange("j i t -> j (i t)"), Gst[:, 1].rearrange("p i t -> p (i t)")
                        ).then_inc(gb_st[1], 16)
            e.wait_ge(gb_st[0], 16 * NTB // 2)
            e.wait_ge(gb_st[1], 16 * NTB // 2)
            e.dma_start(wfin[:], norm_final_w.rearrange("(a n) -> a n", a=1).broadcast_to([P, D])).then_inc(wf_in, 16)
            for x in range(GRP):
                pool_second(e, x, x)
            groups(e, pool_second)

        @block.tensor
        def _(e):
            pe_front(e)
            pe_ssd(e)
            pe_attention(e)
            pe_merge(e)
            pe_routing(e)
            e.wait_ge(sc_out, 2 * P_HEADS)
            pe_turn_u(e, 0, 0)
            pe_turn_u(e, 1, 1)
            for x in range(R_TILES):
                pe_hidden(e, x, x % 4)
            with e.Fori(1, TT) as t:
                for x in range(R_TILES):
                    pe_hidden(e, t * R_TILES + x, x % 4)
                    if x == 1:
                        pe_route(e, t - 1)
            for E in range(R_END, G0):
                pe_hidden(e, E, E % 4)
                if E == R_END + 1:
                    pe_route(e, TT - 1)

            def beside_gates(b2):
                for x in range(G_TILES):
                    pe_hidden(e, b2 * G_TILES + G0 + x, x % 4)
                    pe_gates(e, b2, 2 * x)
                    pe_gates(e, b2, 2 * x + 1)

            beside_gates(0)
            with e.Fori(1, NTB // 2) as b2:
                beside_gates(b2)
            for E in range(G_END, E_TILES):
                pe_hidden(e, E, E % 4, turn=E + 2 < E_TILES)
            e.wait_ge(h_gelu, E_TILES)
            pe_second(e, 0, 0)
            groups(e, lambda e, E, x: pe_second(e, E, x // GRP) if x % GRP == 0 else None)

        @block.scalar
        def _(e):
            o = Ordered(e, aco)
            act_front(e, o)
            act_ssd(e)
            act_attention(e)
            act_pssd(e)
            act_merge(e)
            act_routing(e)
            act_turn_u(e, 0, 0)
            act_turn_u(e, 1, 1)

            def beside_routing(t):
                for x in range(R_TILES):
                    act_hidden(e, t * R_TILES + x, x % 4)
                    if x == R_TILES - 2:
                        act_route(e, t)

            beside_routing(0)
            with e.Fori(1, TT) as t:
                beside_routing(t)
            for E in range(R_END, G0):
                act_hidden(e, E, E % 4)

            def beside_gates(b2):
                for x in range(G_TILES):
                    act_hidden(e, b2 * G_TILES + G0 + x, x % 4)
                    act_gates(e, b2, 2 * x)
                    act_gates(e, b2, 2 * x + 1)

            beside_gates(0)
            with e.Fori(1, NTB // 2) as b2:
                beside_gates(b2)
            for E in range(G_END, E_TILES):
                act_hidden(e, E, E % 4, turn=E + 2 < E_TILES)
                if early(E) is not None:
                    act_second(e, early(E), early(E))
            groups(e, act_second)
            e.wait_ge(o_mm, 2 * E_TILES)
            for t in range(TT):
                e.wait_ge(o_add, 2 * E_TILES - 8 + 2 * (t + 1))
                e.activation(ost[:, t, :], X[:, t, :], ACT.Square, accum_out=stat[:, t:t + 1]).then_inc(f_sq, 1)
                e.wait_ge(f_sq, t + 1)
                e.activation(stat[:, 4 + t:5 + t], stat[:, t:t + 1], ACT.Sqrt, bias=epsc[:, 0:1], scale=1.0 / D
                             ).then_inc(f_rt, 1)

        @block.vector
        def _(e):
            o = Ordered(e, dvo)
            dve_front(e, o)
            dve_ssd(e, o)
            dve_attention(e, o)
            dve_pssd(e)
            dve_merge(e)
            dve_routing(e, o)
            dve_turn_u(e, 0, 0)
            dve_turn_u(e, 1, 1)

            def beside_routing(t):
                pieces = route(e, o, t)
                for x in range(R_TILES):
                    dve_hidden(e, t * R_TILES + x, x % 4)
                    if x == 2 and not (isinstance(t, int) and t == 0):
                        dve_route_out(e, t - 1)
                    spent = 0.0
                    for cost in pieces:
                        spent += cost
                        if spent > ROUTE_WORK / R_TILES and x < R_TILES - 1:
                            break

            o_before = o.n
            beside_routing(0)
            per = o.n - o_before
            with e.Fori(1, TT) as t:
                o.again(t, 1, per)
                beside_routing(t)
            o.over(TT - 1, per)
            for E in range(R_END, G0):
                dve_hidden(e, E, E % 4)
            dve_route_out(e, TT - 1)
            e.wait_ge(r_out, TT)
            o.did(e.tensor_copy(iotab[:], iota[:]))
            o.did(e.tensor_copy(ib16[:], rt[:, 0, :]))
            o.did(e.tensor_copy(jb16[:], rt[:, 1, :]))
            o.then(e.tensor_copy(gb16[:], rt[:, 2, :]))
            o.then(e.tensor_tensor(rest1[:], rt[:, 2, :], gb16[:], ALU.subtract))
            o.then(e.tensor_copy(gb16[:], rest1[:]))
            o.then(e.tensor_tensor(rest2[:], rest1[:], gb16[:], ALU.subtract))

            def beside_gates(b2):
                for x in range(G_TILES):
                    dve_onehots(e, b2, 2 * x)
                    dve_onehots(e, b2, 2 * x + 1)
                    dve_hidden(e, b2 * G_TILES + G0 + x, x % 4)

            beside_gates(0)
            with e.Fori(1, NTB // 2) as b2:
                beside_gates(b2)
            for E in range(G_END, E_TILES):
                dve_hidden(e, E, E % 4, turn=E + 2 < E_TILES)
                if early(E) is not None:
                    dve_second(e, early(E), early(E))
            groups(e, dve_second)
            for n in range(2 * E_TILES - 10, 2 * E_TILES):
                dve_add_output(e, n, n % 8)
            e.wait_ge(wf_in, 16)
            for t in range(TT):
                e.wait_ge(f_rt, t + 1)
                o.then(e.reciprocal(stat[:, 8 + t:9 + t], stat[:, 4 + t:5 + t]))
                e.scalar_tensor_tensor(out=ost[:, t, :], in0=X[:, t, :], scalar=stat[:, 8 + t:9 + t], in1=wfin[:],
                                       op0=ALU.mult, op1=ALU.mult).then_inc(f_out, 1)


_INS = ["x", "positions", "norm_mix_w", "w_in", "conv_w", "conv_b", "dt_bias_fwd", "dt_bias_bwd", "a_log_fwd",
        "a_log_bwd", "d_skip", "ssd_norm_w", "q_a_norm_w", "w_q_b", "kv_a_norm_w", "w_kv_b", "w_proj_ssd",
        "w_proj_mla", "w_out", "norm_ffn_w", "peer_w_q", "peer_sub_keys", "peer_u", "peer_v", "norm_final_w"]


def kernel(**inputs):
    import concourse.bacc as bacc
    from concourse.bass_utils import run_bass_kernel_spmd

    nc = bacc.Bacc("TRN2", target_bir_lowering=False, num_devices=1)
    arrays = {f"in_{n}": np.ascontiguousarray(inputs[n]) for n in _INS}
    exps = np.arange(0, QK_ROPE, 2, dtype=np.float32) / np.float32(QK_ROPE)
    arrays["in_rope_inv"] = (np.float32(1.0) / np.float32(ROPE_THETA) ** exps).astype(np.float32)
    args = [nc.dram_tensor(k, a.shape, mybir.dt.from_np(a.dtype), kind="ExternalInput").ap() for k, a in arrays.items()]
    shape = arrays["in_x"].shape
    out = nc.dram_tensor("out_0", shape, F32, kind="ExternalOutput").ap()
    gates_dram = nc.dram_tensor("gates_dram", (2 * shape[2] // P, P, shape[1]), F32, kind="Internal").ap()
    G_dram = nc.dram_tensor("G_dram", (shape[1] // 32, P, P, 32), F32, kind="Internal").ap()
    act_dram = nc.dram_tensor("act_dram", (arrays["in_peer_u"].shape[0] // P, P, shape[1]), F32, kind="Internal").ap()
    block_kernel(nc, *args, out, gates_dram, G_dram, act_dram)
    r = run_bass_kernel_spmd(nc, [arrays], core_ids=[0])
    return r.results[0]["out_0"]
```
